# Optimizing a Trainium2 kernel written in Bass

```python
import jax, jax.numpy as jnp
from jax import lax
import numpy as np

D_MODEL = 1024
BATCH = 1
SEQ = 256
DEPTH = 2

EPS = 1e-6
SB_HEADS = 8
SB_HEAD_DIM = D_MODEL // 16
SB_WIDTH = SB_HEADS * SB_HEAD_DIM
SB_BLOCK = 128
GLA_HEADS = 4
GLA_DV = D_MODEL // 8
GLA_DK = GLA_DV // 2
GLA_KW = GLA_HEADS * GLA_DK
GLA_VW = GLA_HEADS * GLA_DV
GLA_GATE_RANK = 16
GLA_GATE_NORM = 16.0
GLA_CHUNK = 64
AB_SPLITS = [SB_WIDTH, 2 * SB_WIDTH, 3 * SB_WIDTH,
             3 * SB_WIDTH + GLA_KW, 3 * SB_WIDTH + 2 * GLA_KW,
             3 * SB_WIDTH + 2 * GLA_KW + GLA_VW,
             3 * SB_WIDTH + 2 * GLA_KW + 2 * GLA_VW]
AB_IN = 3 * SB_WIDTH + 2 * GLA_KW + 2 * GLA_VW + GLA_GATE_RANK
AB_MIX = SB_WIDTH + GLA_VW
SGU_WIDTH = 2 * D_MODEL
SGU_GROUPS = 8
SGU_GROUP_DIM = SGU_WIDTH // SGU_GROUPS
SGU_CHUNK = 128
PEER_HEADS = 8
PEER_TOPK = 16
N_KEYS = 128
N_EXPERTS = N_KEYS * N_KEYS
PEER_QDIM = 256
PEER_QHALF = PEER_QDIM // 2
PEER_TOKEN_BLOCK = 128

kernel_name = "hybrid_sb_gla_sgu_peer"

def rmsnorm(x, g):
    xf = x.astype(jnp.float32)
    y = xf * lax.rsqrt(jnp.mean(xf * xf, axis=-1, keepdims=True) + EPS)
    return (y * g.astype(jnp.float32)).astype(x.dtype)

def stick_breaking(q, k, v):
    b_, h_, s_, dh = q.shape
    nb = s_ // SB_BLOCK
    qb = q.astype(jnp.float32).reshape(b_, h_, nb, SB_BLOCK, dh).transpose(2, 0, 1, 3, 4)
    kf = k.astype(jnp.float32)
    vf = v.astype(jnp.float32)
    key_pos = jnp.arange(s_)
    scale = dh ** -0.5

    def one_block(args):
        qi, start = args
        z = jnp.einsum('bhqd,bhkd->bhqk', qi, kf) * scale
        q_pos = start + jnp.arange(SB_BLOCK)
        mask = key_pos[None, :] < q_pos[:, None]
        log_stay = jnp.where(mask, jax.nn.log_sigmoid(-z), 0.0)
        suffix = lax.cumsum(log_stay, axis=3, reverse=True) - log_stay
        a = jnp.where(mask, jnp.exp(jax.nn.log_sigmoid(z) + suffix), 0.0)
        return jnp.einsum('bhqk,bhkd->bhqd', a, vf)

    out = lax.map(one_block, (qb, jnp.arange(nb) * SB_BLOCK))
    return out.transpose(1, 0, 3, 2, 4).reshape(b_, s_, h_ * dh)

def gla(q, k, v, log_a):
    b_, h_, s_, dk = q.shape
    dv = v.shape[-1]
    n = s_ // GLA_CHUNK

    def ch(t):
        return t.reshape(b_, h_, n, GLA_CHUNK, t.shape[-1])

    q, k, v, log_a = ch(q), ch(k), ch(v), ch(log_a)
    bcum = jnp.cumsum(log_a, axis=3)
    q_in = q * (dk ** -0.5) * jnp.exp(bcum)
    k_in = k * jnp.exp(-bcum)
    causal = jnp.tril(jnp.ones((GLA_CHUNK, GLA_CHUNK), dtype=bool))
    scores = jnp.where(causal, jnp.einsum('bhnqd,bhnkd->bhnqk', q_in, k_in), 0.0)
    o_intra = jnp.einsum('bhnqk,bhnke->bhnqe', scores, v)
    b_last = bcum[:, :, :, -1:, :]
    kv = jnp.einsum('bhnkd,bhnke->bhnde', k * jnp.exp(b_last - bcum), v)
    decay = jnp.exp(b_last[:, :, :, 0, :])

    def step(state, inp):
        dec, kv_c = inp
        return dec[..., None] * state + kv_c, state

    init = jnp.zeros((b_, h_, dk, dv), jnp.float32)
    _, prev = lax.scan(step, init, (jnp.moveaxis(decay, 2, 0), jnp.moveaxis(kv, 2, 0)))
    prev = jnp.moveaxis(prev, 0, 2)
    o = o_intra + jnp.einsum('bhnqd,bhnde->bhnqe', q_in, prev)
    return o.reshape(b_, h_, s_, dv)

def layer_ab(h, w_in, w_alpha2, b_alpha2, gla_norm, w_out):
    b_, s_, _ = h.shape
    p = h @ w_in
    q_sb, k_sb, v_sb, q_g, k_g, v_g, g_g, a_lr = jnp.split(p, AB_SPLITS, axis=-1)

    def heads(t, nh):
        return t.reshape(b_, s_, nh, -1).transpose(0, 2, 1, 3)

    o_sb = stick_breaking(heads(q_sb, SB_HEADS), heads(k_sb, SB_HEADS), heads(v_sb, SB_HEADS))

    log_a = jax.nn.log_sigmoid((a_lr @ w_alpha2 + b_alpha2).astype(jnp.float32)) / GLA_GATE_NORM
    f32 = jnp.float32
    o_g = gla(heads(q_g, GLA_HEADS).astype(f32), heads(k_g, GLA_HEADS).astype(f32),
              heads(v_g, GLA_HEADS).astype(f32), heads(log_a, GLA_HEADS))
    o_g = o_g * lax.rsqrt(jnp.mean(o_g * o_g, axis=-1, keepdims=True) + EPS)
    o_g = o_g.transpose(0, 2, 1, 3).reshape(b_, s_, GLA_VW) * gla_norm.astype(f32)
    o_g = o_g * jax.nn.silu(g_g.astype(f32))

    mix = jnp.concatenate([o_sb, o_g], axis=-1).astype(h.dtype)
    return mix @ w_out

def layer_c(h, w_in, v_norm, w_spatial, b_spatial, w_out):
    b_, s_, _ = h.shape
    n = s_ // SGU_CHUNK
    z = jax.nn.gelu(h @ w_in, approximate=False)
    u, v = jnp.split(z, 2, axis=-1)
    v = rmsnorm(v, v_norm).reshape(b_, n, SGU_CHUNK, SGU_GROUPS, SGU_GROUP_DIM)
    causal = jnp.tril(jnp.ones((SGU_CHUNK, SGU_CHUNK), dtype=bool))
    w = jnp.where(causal[None], w_spatial, 0.0)
    mixed = jnp.einsum('gts,bnsgc->bntgc', w, v) + b_spatial.T[:, :, None]
    return (u * mixed.reshape(b_, s_, SGU_WIDTH)) @ w_out

def peer(h, w_q, subkeys, u_tab, v_tab):
    b_, s_, d = h.shape
    t_ = b_ * s_
    hf = h.reshape(t_, d)
    q = (hf @ w_q).astype(jnp.float32).reshape(t_, PEER_HEADS, 2, PEER_QHALF)
    scores = jnp.einsum('thpd,hpnd->thpn', q, subkeys.astype(jnp.float32))
    top_s, top_i = lax.top_k(scores, PEER_TOPK)
    cand_s = (top_s[:, :, 0, :, None] + top_s[:, :, 1, None, :]).reshape(t_, PEER_HEADS, -1)
    cand_i = (top_i[:, :, 0, :, None] * N_KEYS + top_i[:, :, 1, None, :]).reshape(t_, PEER_HEADS, -1)
    best_s, pos = lax.top_k(cand_s, PEER_TOPK)
    idx = jnp.take_along_axis(cand_i, pos, axis=-1)
    gate = jax.nn.softmax(best_s, axis=-1)

    nblk = t_ // PEER_TOKEN_BLOCK
    xb = hf.reshape(nblk, PEER_TOKEN_BLOCK, d)
    ib = idx.reshape(nblk, PEER_TOKEN_BLOCK, PEER_HEADS * PEER_TOPK)
    gb = gate.reshape(nblk, PEER_TOKEN_BLOCK, PEER_HEADS * PEER_TOPK)

    def expert_block(args):
        xi, ii, gi = args
        u_sel = u_tab[ii]
        act = jax.nn.gelu(jnp.einsum('td,tkd->tk', xi, u_sel).astype(jnp.float32), approximate=False)
        w = (gi * act).astype(v_tab.dtype)
        return jnp.einsum('tk,tkd->td', w, v_tab[ii])

    out = lax.map(expert_block, (xb, ib, gb))
    return out.reshape(b_, s_, d).astype(h.dtype)

def setup_inputs(seed: int = 0) -> dict:
    key = jax.random.key(seed)
    ks = jax.random.split(key, 20)
    n_even = (DEPTH + 1) // 2
    n_odd = DEPTH // 2
    nrm = jax.random.normal
    f32 = jnp.float32
    return {
        "x": nrm(ks[0], (BATCH, SEQ, D_MODEL), f32),
        "norm_mix": 1.0 + 0.02 * nrm(ks[1], (DEPTH, D_MODEL), f32),
        "norm_ffn": 1.0 + 0.02 * nrm(ks[2], (DEPTH, D_MODEL), f32),
        "ab_w_in": nrm(ks[3], (n_even, D_MODEL, AB_IN), f32) * D_MODEL ** -0.5,
        "ab_w_alpha2": nrm(ks[4], (n_even, GLA_GATE_RANK, GLA_KW), f32) * GLA_GATE_RANK ** -0.5,
        "ab_b_alpha2": 0.1 * nrm(ks[5], (n_even, GLA_KW), f32),
        "ab_gla_norm": 1.0 + 0.02 * nrm(ks[6], (n_even, GLA_VW), f32),
        "ab_w_out": nrm(ks[7], (n_even, AB_MIX, D_MODEL), f32) * AB_MIX ** -0.5,
        "c_w_in": nrm(ks[8], (n_odd, D_MODEL, 2 * SGU_WIDTH), f32) * D_MODEL ** -0.5,
        "c_v_norm": 1.0 + 0.02 * nrm(ks[9], (n_odd, SGU_WIDTH), f32),
        "c_w_spatial": nrm(ks[10], (n_odd, SGU_GROUPS, SGU_CHUNK, SGU_CHUNK), f32) * SGU_CHUNK ** -0.5,
        "c_b_spatial": 1.0 + 0.02 * nrm(ks[11], (n_odd, SGU_GROUPS, SGU_CHUNK), f32),
        "c_w_out": nrm(ks[12], (n_odd, SGU_WIDTH, D_MODEL), f32) * SGU_WIDTH ** -0.5,
        "peer_w_q": nrm(ks[13], (DEPTH, D_MODEL, PEER_HEADS * PEER_QDIM), f32) * D_MODEL ** -0.5,
        "peer_subkeys": nrm(ks[14], (DEPTH, PEER_HEADS, 2, N_KEYS, PEER_QHALF), f32) * PEER_QHALF ** -0.5,
        "peer_u": nrm(ks[15], (DEPTH, N_EXPERTS, D_MODEL), f32) * D_MODEL ** -0.5,
        "peer_v": nrm(ks[16], (DEPTH, N_EXPERTS, D_MODEL), f32) * PEER_HEADS ** -0.5,
        "final_norm": 1.0 + 0.02 * nrm(ks[17], (D_MODEL,), f32),
    }

def reference(x, norm_mix, norm_ffn, ab_w_in, ab_w_alpha2, ab_b_alpha2, ab_gla_norm, ab_w_out,
              c_w_in, c_v_norm, c_w_spatial, c_b_spatial, c_w_out,
              peer_w_q, peer_subkeys, peer_u, peer_v, final_norm):
    for i in range(DEPTH):
        j = i // 2
        h = rmsnorm(x, norm_mix[i])
        if i % 2 == 0:
            x = x + layer_ab(h, ab_w_in[j], ab_w_alpha2[j], ab_b_alpha2[j], ab_gla_norm[j], ab_w_out[j])
        else:
            x = x + layer_c(h, c_w_in[j], c_v_norm[j], c_w_spatial[j], c_b_spatial[j], c_w_out[j])
        x = x + peer(rmsnorm(x, norm_ffn[i]), peer_w_q[i], peer_subkeys[i], peer_u[i], peer_v[i])
    return rmsnorm(x, final_norm)


_drawn_inputs = setup_inputs


def setup_inputs(seed=0):
    import zlib

    import numpy as np

    out = dict(_drawn_inputs(seed))
    spreads = {}
    factors = {}
    for name, (base, spread) in spreads.items():
        noise = np.random.default_rng([zlib.crc32(name.encode()), seed]).standard_normal(out[name].shape)
        drawn = base * np.exp(spread * noise) if base else spread * noise
        out[name] = __import__('jax').numpy.asarray(drawn.astype(out[name].dtype))
    for name, factor in factors.items():
        out[name] = (out[name] * factor).astype(out[name].dtype)
    return out
```

```python
import concourse.bass as bass
from concourse import mybir
from collections import namedtuple
from contextlib import ExitStack

P = 128
NBLK = 2
T = P * NBLK
D = 1024
KT = D // P
CH = 512
EPS = 1e-6
SBH, SBD = 8, 64
GH, GDK, GDV, GC = 4, 64, 128, 64
RANK = 16
GATE_NORM = 16.0
SGW, SGG, SGC = 2048, 8, 256
PH, TOPK, NK = 8, 16, 128
NE = PH * TOPK
NEG = -1.0e30
LOWEST = -3.0e38

STEPS = 8
HALF = STEPS // 2
TURNS = NE // STEPS
WB = 4


B_HT, B_Q, B_K, B_V, B_GQ, B_GK, B_GV, B_GG = 0, 4, 6, 8, 10, 11, 12, 14
B_RANK, B_ALPHA, B_KD, B_KV, B_GS, B_GO, B_GT = 16, 17, 18, 20, 23, 25, 27
B_Z = [29] + [28 + 2 * hd for hd in range(1, SBH)]
B_E = [31 + 2 * hd for hd in range(SBH - 1)] + [29 + 2 * SBH - 1]
B_SO = B_E[-1] + 1
B_OUT = B_SO + 2
MIX0_BANKS = B_OUT + 2 * NBLK
N_CONSTS = 5
N_MASKS = 19
VNORM_COL = 14


def banks_of(stage):
    kind, args = stage[0], stage[1:]
    return {"MIX0": lambda: MIX0_BANKS, "SPATIAL": lambda: 2, "QNORM": lambda: 2 * len(args[1]),
            "QKEYS": lambda: 4, "QSCORE": lambda: 2 * len(args[1]), "ZNORM": lambda: 2,
            "ZPROJ": lambda: 1, "MIXG": lambda: 4, "MIXT": lambda: 4, "MIXO": lambda: 1,
            }.get(kind, lambda: 0)()


def chunks_of(stage):
    return {"MIX0": 8, "QSCORE": 1, "ZPROJ": 1, "MIXO": 2}.get(stage[0], 0)


def peer_scores(layer, blocks):
    return ([("QNORM", layer, blocks), ("QKEYS", layer)]
            + [("QSCORE", layer, blocks, m) for m in range(4)])


def topk(layer, b):
    return [("TOPK", layer, b, part) for part in range(4)]


def mixer1(b):
    return ([("ZNORM", b)] + [("ZPROJ", b, j) for j in (4, 5, 6, 7)] + [("VNORM", b)]
            + [("ZPROJ", b, j) for j in (0, 1, 2, 3)] + [("MIXG", b), ("MIXT", b)]
            + [("MIXO", b, n) for n in range(2)])


def gather_with(layer, b, others):
    cuts = min(TURNS, len(others) + 1) if others else 1
    out, at, done = [("ACC", layer, b)], 0, 0
    for c in range(cuts):
        end = TURNS * (c + 1) // cuts
        out.append(("GATHER", layer, b, at, end))
        at = end
        upto = len(others) * (c + 1) // (cuts - 1) if cuts > 1 and c < cuts - 1 else len(others)
        out += others[done:upto]
        done = upto
    return out + [("ADD", layer, b)]


PLAN = ([("MIX0",), ("SPATIAL",)] + peer_scores(0, (0, 1)) + topk(0, 0)
        + gather_with(0, 0, topk(0, 1))
        + gather_with(0, 1, mixer1(0) + peer_scores(1, (0,)) + topk(1, 0))
        + gather_with(1, 0, mixer1(1) + peer_scores(1, (1,)) + topk(1, 1))
        + gather_with(1, 1, [("FINAL", 0)]) + [("FINAL", 1)])


Place = namedtuple("Place", "bank chunk x_writes nat gain")


def walk():
    bank = chunk = x_writes = nat = gain = 0
    for stage in PLAN:
        kind = stage[0]
        yield kind, stage[1:], Place(bank, chunk, x_writes, nat, gain)
        bank += banks_of(stage)
        chunk += chunks_of(stage)
        x_writes += NBLK if kind == "MIX0" else kind == "ADD" or (kind == "MIXO" and stage[2] == 1)
        nat += kind in ("SPATIAL", "QKEYS", "ZNORM")
        gain += kind in ("MIX0", "QNORM", "ZNORM", "FINAL")


def trunk(nc, x_in, norm_mix, norm_ffn, ab_w_in, ab_w_alpha2, ab_b_alpha2, ab_gla_norm, ab_w_out,
          c_w_in, c_v_norm, c_w_spatial, c_b_spatial, c_w_out,
          peer_w_q, peer_subkeys, peer_u, peer_v, final_norm, out):
    f32, i32, u32 = mybir.dt.float32, mybir.dt.int32, mybir.dt.uint32
    ALU = mybir.AluOpType
    ACT = mybir.ActivationFunctionType
    AX = mybir.AxisListType
    ctx = ExitStack()
    with ctx:
        def sb(name, shape, dt=f32):
            return ctx.enter_context(nc.sbuf_tensor(name, shape, dt))

        def sem(name):
            return ctx.enter_context(nc.semaphore(name))

        x = sb("x", [P, NBLK, D])
        h = sb("h", [P, NBLK, D])
        hT = sb("hT", [P, KT, T])
        mixT = sb("mixT", [P, KT, T])
        weights = sb("weights", [P, 2, KT, CH])
        ring = sb("ring", [P, 2 * STEPS, D])
        z = sb("z", [P, 2 * SGW])
        scores = sb("scores", [P, 2 * PH * NK])
        gain = sb("gain", [P, 2, D])
        nat = sb("nat", [P, 2 * PH * NK])
        keysT = sb("keysT", [P, 2 * PH, NK])
        spatialT = sb("spatialT", [P, SGG, P])
        queries = sb("queries", [P, 2, CH])
        diag = sb("diag", [P, STEPS, P])
        ident = sb("ident", [P, P])
        digits = sb("digits", [P, TOPK])
        b_spatial = sb("b_spatial", [P, SGG])
        b_alpha = sb("b_alpha", [P, 2])
        w_alpha = sb("w_alpha", [RANK, GH * GDK])
        w_rank = sb("w_rank", [P, KT, RANK])
        squares = sb("squares", [P, 16])
        roots = sb("roots", [P, 2, 16])
        scale = sb("scale", [P, 16])
        gla_stat = sb("gla_stat", [P, 3, NBLK * GH])
        alphaT = sb("alphaT", [RANK, T])
        top = sb("top", [P, 2 * PH, TOPK])
        topi = sb("topi", [P, 2 * PH, TOPK], u32)
        topf = sb("topf", [P, 2 * PH, TOPK])
        best = sb("best", [P, PH, TOPK])
        where = sb("where", [P, PH, TOPK], u32)
        digit = sb("digit", [P, 2, NE], u32)
        digitf = sb("digitf", [P, 2, NE])
        picked = sb("picked", [P, 2, NE])
        gsum = sb("gsum", [P, 2, PH])
        experts = sb("experts", [P, NBLK, NE], i32)
        gates = sb("gates", [P, NBLK, NE])
        idx = sb("idx", [P, STEPS], i32)
        dots = sb("dots", [P, STEPS])
        gelus = sb("gelus", [P, STEPS])
        wts = sb("wts", [P, STEPS])

        acc = [ctx.enter_context(nc.psum_tensor(f"acc{k}", [P, CH], f32)) for k in range(4)]
        work = [ctx.enter_context(nc.psum_tensor(f"work{k}", [P, CH], f32)) for k in range(WB)]

        def slots(k, n=1):
            return ring[:, k:k + n, :].rearrange("p a b -> p (a b)")

        suffix = slots(9)[:, 768:768 + 2 * P].rearrange("p (a b) -> p a b", a=2)
        before = slots(8)[:, 512:512 + 3 * P].rearrange("p (a b) -> p a b", a=3)
        beyond = queries[:, 0, 0:3 * P].rearrange("p (a b) -> p a b", a=3)
        chunk_mask = slots(8)[:, 896:896 + P]
        resets = slots(10)[:, 768:768 + T]
        gla_gain = queries[:, 1, :]
        qT = slots(0).rearrange("p (j t) -> p j t", t=T)
        kz = slots(1, 2).rearrange("p (j t) -> p j t", t=T)
        v_sb = slots(3).rearrange("p (b n) -> p b n", b=NBLK)
        AT = slots(4, 3).rearrange("p (j t) -> p j t", t=3 * P)
        qz = slots(7).rearrange("p (j t) -> p j t", t=T)
        kin = slots(8)[:, 0:2 * T].rearrange("p (j t) -> p j t", t=T)
        kdz = slots(9)[:, 0:768].rearrange("p (c j t) -> p c j t", c=3, j=2)
        kd = slots(10)[:, 0:768].rearrange("p (c j t) -> p c j t", c=3, j=2)
        state = slots(11)[:, 0:768].rearrange("p (c j t) -> p c j t", c=3, j=2)
        v_g = slots(12).rearrange("p (b n) -> p b n", b=NBLK)
        gg = slots(13).rearrange("p (b n) -> p b n", b=NBLK)
        og = slots(14).rearrange("p (b n) -> p b n", b=NBLK)
        scT = slots(15).rearrange("p (b j t) -> p b j t", b=NBLK, j=GH)
        za, t1, la, bc = (scores[:, k * CH:(k + 1) * CH] for k in range(4))
        eb, enb, edec = (z[:, k * CH:(k + 1) * CH] for k in range(3))
        stick = z[:, 1536:1536 + 6 * 384].rearrange("p (k s t) -> p k s t", k=3, s=2)
        mixT1 = mixT[:, :, :].rearrange("p a b -> p (a b)").rearrange("p (k t) -> p k t", t=P)

        full = [sem(f"bank_full{k}") for k in range(WB)]
        free = [sem(f"bank_free{k}") for k in range(WB)]
        chunk_in = [sem(f"chunk_in{k}") for k in range(2)]
        half_used = sem("half_used")
        x_in_sem = sem("x_in")
        consts_in = sem("consts_in")
        gain_in = [sem(f"gain_in{k}") for k in range(2)]
        nat_in = sem("nat_in")
        masks = sem("masks")
        nat_masked = sem("nat_masked")
        x_ready = sem("x_ready")
        sq_ready = sem("sq_ready")
        mean_ready = sem("mean_ready")
        root_ready = sem("root_ready")
        h_ready = sem("h_ready")
        act_link = sem("act_link")
        dve_link = sem("dve_link")
        act_out = sem("act_out")
        dve_out = sem("dve_out")
        experts_ready = sem("experts_ready")
        gates_ready = sem("gates_ready")
        gla_in = sem("gla_in")
        gla_states = sem("gla_states")
        soft_ready = sem("soft_ready")
        log_ready = sem("log_ready")
        exp_ready = sem("exp_ready")
        prob_ready = sem("prob_ready")
        v_ready = sem("v_ready")
        u_in = [sem(f"u_in{k}") for k in range(STEPS)]
        v_in = [sem(f"v_in{k}") for k in range(STEPS)]
        dots_done = sem("dots_done")
        v_used = sem("v_used")
        gelu_done = sem("gelu_done")
        wts_ready = sem("wts_ready")
        diag_ready = sem("diag_ready")
        idx_copied = sem("idx_copied")
        pool_turn = sem("pool_turn")
        stored = sem("stored")

        def await_bank(eng, n):
            eng.wait_ge(full[n % WB], n // WB + 1)
            return work[n % WB]

        def claim_bank(eng, n):
            if n >= WB:
                eng.wait_ge(free[n % WB], n // WB)
            return work[n % WB]

        def await_chunk(eng, n):
            eng.wait_ge(chunk_in[n % 2], 16 * (n // 2 + 1))
            return weights[:, n % 2]

        def gather_turn(layer, b):
            return (2 * layer + b) * TURNS

        def score_rows(layer, b):
            return z[:, 0:2 * PH * NK] if (layer, b) == (0, 1) else scores[:, :]

        def halves(bank, n=2):
            return bank[:, :].rearrange("p (j t) -> p j t", j=n)

        u_rows = peer_u.rearrange("l e d -> (l e) d")
        v_rows = peer_v.rearrange("l e d -> (l e) d")

        block = ctx.enter_context(nc.Block())

        @block.sync
        def _(sp):
            def tiled(w, r0, c0, cols=CH):
                return w[r0:r0 + D, c0:c0 + cols].rearrange("(k p) n -> p k n", p=P)

            norms = [0]
            chunk_free = []
            nat_free = [None]

            def filled(n):
                return full[n % WB], n // WB + 1

            def load_chunk(n, src, used):
                if n >= 2:
                    sp.wait_ge(*chunk_free[n - 2])
                sp.dma_start(weights[:, n % 2, :, :], src).then_inc(chunk_in[n % 2], 16)
                chunk_free.append(used)

            def load_gain(g, src, n):
                if g >= 2:
                    sp.wait_ge(h_ready, norms[g - 1])
                sp.dma_start(gain[:, g % 2, :], src.partition_broadcast(P)).then_inc(gain_in[g % 2], 16)
                norms.append(norms[-1] + n)

            def load_nat(dst, src, used):
                if nat_free[0]:
                    sp.wait_ge(*nat_free[0])
                sp.dma_start(dst, src).then_inc(nat_in, 16)
                nat_free[0] = used

            halves_used = v_norms = 0
            sp.dma_start(w_rank[:, :, :], tiled(ab_w_in[0], 0, 6 * CH, RANK)).then_inc(consts_in, 16)
            for kind, args, at in walk():
                bank, chunk = at.bank, at.chunk
                if kind == "MIX0":
                    load_gain(at.gain, norm_mix[0], NBLK)
                    for j, last in enumerate((B_Q + 1, B_K + 1, B_V + 1, B_GK, B_GV + 1, B_GG + 1)):
                        load_chunk(chunk + j, tiled(ab_w_in[0], 0, j * CH), filled(bank + last))
                    for n in range(2):
                        load_chunk(chunk + 6 + n, tiled(ab_w_out[0], 0, n * CH), filled(bank + B_OUT + 2 * n + 1))
                elif kind == "SPATIAL":
                    load_nat(nat[:, 0:SGG * P].rearrange("t (g s) -> t g s", g=SGG),
                             c_w_spatial[0].rearrange("g t s -> t g s"), filled(bank + 1))
                elif kind == "QNORM":
                    load_gain(at.gain, norm_ffn[args[0]], len(args[1]))
                elif kind == "QKEYS":
                    load_nat(nat[:, :].rearrange("n (g d) -> n g d", d=NK),
                             peer_subkeys[args[0]].rearrange("h q n d -> n (h q) d"), filled(bank + 3))
                elif kind == "QSCORE":
                    load_chunk(chunk, tiled(peer_w_q[args[0]], 0, args[2] * CH), filled(bank + 2 * len(args[1]) - 2))
                elif kind == "ZNORM":
                    v_norms += 1
                    load_gain(at.gain, norm_mix[1], 1)
                    load_nat(nat[:, :], c_v_norm[0].partition_broadcast(P), (v_ready, v_norms))
                elif kind == "ZPROJ":
                    load_chunk(chunk, tiled(c_w_in[0], 0, args[1] * CH), filled(bank))
                elif kind == "MIXO":
                    halves_used += 1
                    for kh in range(2):
                        load_chunk(chunk + kh, tiled(c_w_out[0], kh * D, args[1] * CH),
                                   filled(bank) if kh else (half_used, halves_used))
                elif kind == "FINAL":
                    load_gain(at.gain, final_norm, 1)
                    sp.wait_ge(h_ready, norms[-1])
                    sp.dma_start(out[0, args[0] * P:(args[0] + 1) * P, :], h[:, args[0], :]).then_inc(stored, 16)
            sp.wait_ge(stored, 16 * NBLK)

        @block.gpsimd
        def _(pool):
            step = [0]

            def after(ins):
                step[0] += 1
                ins.then_inc(masks, 1)

            for tile, value in ((ident[:, :], 0.0), (suffix, -1.0), (before, 1.0), (beyond, 0.0), (chunk_mask, 1.0),
                                (resets, 1.0)):
                after(pool.memset(tile, value))
            for tile in (kz, qz, kdz):
                after(pool.memset(tile, 0.0))
            pool.wait_ge(masks, step[0])
            after(pool.affine_select(out=ident[:, :], in_=ident[:, :], compare_op=ALU.not_equal, fill=1.0,
                                     base=0, pattern=[[-1, P]], channel_multiplier=1))
            after(pool.affine_select(out=suffix[:, 0, :], in_=suffix[:, 0, :], compare_op=ALU.is_ge, fill=0.0,
                                     base=0, pattern=[[-1, P]], channel_multiplier=1))
            for part in (0, 2):
                after(pool.affine_select(out=before[:, part, :], in_=before[:, part, :], compare_op=ALU.is_gt,
                                         fill=0.0, base=0, pattern=[[1, P]], channel_multiplier=-1))
                after(pool.affine_select(out=beyond[:, part, :], in_=beyond[:, part, :], compare_op=ALU.is_gt,
                                         fill=NEG, base=0, pattern=[[1, P]], channel_multiplier=-1))
            after(pool.affine_select(out=chunk_mask[:, :], in_=chunk_mask[:, :], compare_op=ALU.is_ge,
                                     fill=0.0, base=0, pattern=[[1, P]], channel_multiplier=-1))
            after(pool.affine_select(out=resets[:, :].rearrange("p (c t) -> p c t", t=GC),
                                     in_=resets[:, :].rearrange("p (c t) -> p c t", t=GC),
                                     compare_op=ALU.not_equal, fill=0.0, base=0,
                                     pattern=[[0, T // GC], [1, GC]], channel_multiplier=0))
            after(pool.iota(digits[:, :], pattern=[[1, TOPK]], base=0, channel_multiplier=0,
                            allow_small_or_imprecise_dtypes=True))
            pool.wait_ge(masks, step[0])
            after(pool.memset(chunk_mask[0:GC, GC:P], 0.0))
            assert step[0] == N_MASKS

            for kind, args, at in walk():
                bank, chunk = at.bank, at.chunk
                if kind == "SPATIAL":
                    pool.wait_ge(nat_in, 16)
                    m = nat[:, 0:SGG * P].rearrange("t (g s) -> t g s", g=SGG)
                    pool.affine_select(out=m, in_=m, compare_op=ALU.is_ge, fill=0.0, base=0,
                                       pattern=[[0, SGG], [-1, P]], channel_multiplier=1).then_inc(nat_masked, 1)
                elif kind == "GATHER":
                    layer, b, i0, i1 = args
                    t0 = gather_turn(layer, b)
                    pool.wait_ge(experts_ready, 2 * layer + b + 1)
                    with pool.Fori(i0, i1) as i:
                        for g in range(2):
                            now = 2 * (t0 + i) + g + 1
                            pool.wait_ge(dots_done, now)
                            pool.sem_inc(pool_turn, 1)
                            pool.wait_ge(v_used, now)
                            pool.sem_inc(pool_turn, 1)
                            pool.tensor_copy(idx[:, g * HALF:(g + 1) * HALF],
                                             experts[:, b, bass.ds(i * STEPS + g * HALF, HALF)]).then_inc(idx_copied, 1)
                            pool.wait_ge(idx_copied, now)
                            pool.sem_inc(pool_turn, 1)
                            for table, landed, base in ((u_rows, u_in, 0), (v_rows, v_in, STEPS)):
                                for k in range(g * HALF, (g + 1) * HALF):
                                    pool.indirect_dma_start(
                                        ring[:, base + k, :], None, table,
                                        bass.IndirectOffsetOnAxis(ap=idx[:, k:k + 1], axis=0)).then_inc(landed[k], 16)

        @block.scalar
        def _(act):
            links = [0]
            seen = {"dve": 0, "norm": 0}

            def link(ins):
                links[0] += 1
                ins.then_inc(act_link, 1)
                act.wait_ge(act_link, links[0])

            def await_dve():
                seen["dve"] += 1
                act.wait_ge(dve_out, seen["dve"])

            def norm(b, x_writes):
                k = seen["norm"]
                seen["norm"] += 1
                if k < NBLK:
                    act.wait_ge(x_in_sem, 16)
                else:
                    act.wait_ge(x_ready, x_writes)
                nc.scalar.activation(h[:, b, :], x[:, b, :], ACT.Square,
                                     accum_out=squares[:, k:k + 1]).then_inc(sq_ready, 1)
                act.wait_ge(mean_ready, k + 1)
                nc.scalar.activation(roots[:, 1, k:k + 1], roots[:, 0, k:k + 1], ACT.Sqrt).then_inc(root_ready, 1)

            def take_hT(n, b):
                for half in range(2):
                    w = await_bank(act, n + half)
                    nc.scalar.activation(hT[:, half * 4:half * 4 + 4, b * P:(b + 1) * P], halves(w, 4), ACT.Copy)\
                        .then_inc(free[(n + half) % WB], 1)

            act.dma_start(x[:, :, :], x_in[0].rearrange("(b p) d -> p b d", p=P)).then_inc(x_in_sem, 16)
            act.dma_start(w_alpha[:, :], ab_w_alpha2[0]).then_inc(consts_in, 16)
            act.dma_start(b_alpha[:, :], ab_b_alpha2[0].rearrange("(j p) -> p j", p=P),
                          allow_slow_non_contiguous=True).then_inc(consts_in, 16)
            act.dma_start(gla_gain[:, :], ab_gla_norm[0].partition_broadcast(P)).then_inc(consts_in, 16)
            act.dma_start(b_spatial[:, :], c_b_spatial[0].rearrange("g t -> t g"),
                          allow_slow_non_contiguous=True).then_inc(consts_in, 16)

            def mix0(n0):
                for b in range(NBLK):
                    norm(b, 0)
                for b in range(NBLK):
                    take_hT(n0 + 2 * b, b)
                n = n0 + B_Q
                for j in range(2):
                    w = await_bank(act, n + j)
                    nc.scalar.activation(qT[:, 2 * j:2 * j + 2, :], halves(w), ACT.Copy, scale=SBD ** -0.5)\
                        .then_inc(free[(n + j) % WB], 1)
                for dst, at in ((v_sb, n0 + B_V), (v_g, n0 + B_GV)):
                    for b in range(NBLK):
                        w = await_bank(act, at + b)
                        nc.scalar.activation(dst[:, b, :], w[:, :], ACT.Copy).then_inc(free[(at + b) % WB], 1)
                for b in range(NBLK):
                    w = await_bank(act, n0 + B_GG + b)
                    nc.scalar.activation(gg[:, b, :], w[:, :], ACT.Exp, scale=-1.0).then_inc(act_out, 1)

            def mix0_gla(n0):
                w = await_bank(act, n0 + B_RANK)
                nc.scalar.activation(alphaT[:, :], w[0:RANK, 0:T], ACT.Copy).then_inc(free[(n0 + B_RANK) % WB], 1)
                w = await_bank(act, n0 + B_ALPHA)
                act.wait_ge(consts_in, 16 * 5)
                for j in range(2):
                    last = nc.scalar.activation(za[:, j * T:(j + 1) * T], w[:, j * T:(j + 1) * T], ACT.Identity,
                                                bias=b_alpha[:, j:j + 1])
                link(last)
                act.sem_inc(free[(n0 + B_ALPHA) % WB], 1)
                link(nc.scalar.activation(t1, za, ACT.Abs))
                link(nc.scalar.activation(t1, t1, ACT.Exp, scale=-1.0))
                nc.scalar.activation(t1, t1, ACT.Ln, bias=1.0).then_inc(act_out, 1)
                await_dve()
                nc.scalar.activation(eb, bc, ACT.Exp, scale=1.0 / GATE_NORM)
                nc.scalar.activation(enb, bc, ACT.Exp, scale=-1.0 / GATE_NORM)
                nc.scalar.activation(edec, t1, ACT.Exp, scale=1.0 / GATE_NORM).then_inc(act_out, 1)
                for k in range(2):
                    w = await_bank(act, n0 + B_KD + k)
                    n = 4 if k == 0 else 2
                    dst = kd[:, 2 * k:2 * k + n // 2].rearrange("p c j t -> p (c j t)")
                    nc.scalar.activation(dst, w[:, 0:n * P], ACT.Copy).then_inc(free[(n0 + B_KD + k) % WB], 1)
                for b in range(NBLK):
                    w = await_bank(act, n0 + B_GO + b)
                    for hd in range(GH):
                        last = nc.scalar.activation(og[:, b, hd * GDV:(hd + 1) * GDV], w[:, hd * GDV:(hd + 1) * GDV],
                                                    ACT.Square, accum_out=gla_stat[:, 0, b * GH + hd:b * GH + hd + 1])
                    last.then_inc(act_out, 1)
                await_dve()
                nc.scalar.activation(gla_stat[:, 2, :], gla_stat[:, 1, :], ACT.Sqrt).then_inc(act_out, 1)
                for b in range(NBLK):
                    w = await_bank(act, n0 + B_GT + b)
                    nc.scalar.activation(mixT[:, 4:8, b * P:(b + 1) * P], halves(w, 4), ACT.Copy)\
                        .then_inc(free[(n0 + B_GT + b) % WB], 1)

            def stick_soft(n, hd):
                w = await_bank(act, n)
                s = stick[:, 0, hd % 2, :]
                if hd >= 2:
                    act.wait_ge(log_ready, hd - 1)
                link(nc.scalar.activation(s, w[:, 0:3 * P], ACT.Abs))
                link(nc.scalar.activation(s, s, ACT.Exp, scale=-1.0))
                nc.scalar.activation(s, s, ACT.Ln, bias=1.0).then_inc(soft_ready, 1)

            def stick_prob(hd):
                act.wait_ge(exp_ready, hd + 1)
                nc.scalar.activation(AT[:, hd, :], stick[:, 2, hd % 2, :], ACT.Exp).then_inc(prob_ready, 1)

            for kind, args, at in walk():
                bank, chunk = at.bank, at.chunk
                if kind == "MIX0":
                    mix0(bank)
                    mix0_gla(bank)
                    stick_soft(bank + B_Z[0], 0)
                    for hd in range(SBH):
                        if hd + 1 < SBH:
                            stick_soft(bank + B_Z[hd + 1], hd + 1)
                        stick_prob(hd)
                    for k in range(2):
                        n = bank + B_SO + k
                        w = await_bank(act, n)
                        nc.scalar.activation(mixT[:, 2 * k:2 * k + 2, :], halves(w), ACT.Copy).then_inc(free[n % WB], 1)
                elif kind == "SPATIAL":
                    for k in range(2):
                        w = await_bank(act, bank + k)
                        nc.scalar.activation(spatialT[:, 4 * k:4 * k + 4, :], halves(w, 4), ACT.Copy)\
                            .then_inc(free[(bank + k) % WB], 1)
                elif kind == "QNORM":
                    for b in args[1]:
                        norm(b, at.x_writes)
                    for k, b in enumerate(args[1]):
                        take_hT(bank + 2 * k, b)
                elif kind == "QKEYS":
                    for k in range(4):
                        w = await_bank(act, bank + k)
                        nc.scalar.activation(keysT[:, 4 * k:4 * k + 4, :], halves(w, 4), ACT.Copy)\
                            .then_inc(free[(bank + k) % WB], 1)
                elif kind == "QSCORE":
                    layer, blocks, m = args
                    for k, b in enumerate(blocks):
                        n = bank + 2 * k
                        w = await_bank(act, n)
                        nc.scalar.activation(queries[:, n // 2 % 2, :], w[:, :], ACT.Copy).then_inc(free[n % WB], 1)
                        w = await_bank(act, n + 1)
                        dst = score_rows(layer, b)[:, m * CH:(m + 1) * CH]
                        nc.scalar.activation(dst, w[:, :], ACT.Copy).then_inc(free[(n + 1) % WB], 1)
                elif kind == "TOPK":
                    if args[2] == 3:
                        await_dve()
                        nc.scalar.activation(gates[:, args[1], :], gates[:, args[1], :], ACT.Exp).then_inc(act_out, 1)
                elif kind == "GATHER":
                    layer, b, i0, i1 = args
                    t0 = gather_turn(layer, b)
                    with act.Fori(i0, i1) as i:
                        for g in range(2):
                            now = 2 * (t0 + i) + g + 1
                            part = slice(g * HALF, (g + 1) * HALF)
                            act.wait_ge(dots_done, now + 2)
                            nc.scalar.activation(gelus[:, part], dots[:, part], ACT.Gelu).then_inc(gelu_done, 1)
                            act.wait_ge(wts_ready, now)
                            act.wait_ge(v_used, now)
                            for k in range(g * HALF, (g + 1) * HALF):
                                last = nc.scalar.activation(diag[:, k, :], ident[:, :], ACT.Copy, scale=wts[:, k:k + 1])
                            last.then_inc(diag_ready, 1)
                elif kind == "ZNORM":
                    norm(args[0], at.x_writes)
                    take_hT(bank, args[0])
                elif kind == "ZPROJ":
                    w = await_bank(act, bank)
                    cols = slice(args[1] * CH, (args[1] + 1) * CH)
                    nc.scalar.activation(z[:, cols], w[:, :], ACT.Gelu).then_inc(free[bank % WB], 1)
                elif kind == "VNORM":
                    for j in range(4):
                        act.wait_ge(free[(bank - 4 + j) % WB], (bank - 4 + j) // WB + 1)
                    nc.scalar.activation(mixT[:, :, :].rearrange("p a b -> p (a b)"), z[:, SGW:2 * SGW], ACT.Square,
                                         accum_out=squares[:, VNORM_COL + args[0]:VNORM_COL + args[0] + 1]).then_inc(act_out, 1)
                    await_dve()
                    nc.scalar.activation(roots[:, 1, VNORM_COL + args[0]:VNORM_COL + args[0] + 1], roots[:, 0, VNORM_COL + args[0]:VNORM_COL + args[0] + 1],
                                         ACT.Sqrt).then_inc(act_out, 1)
                elif kind == "MIXT":
                    for k in range(4):
                        w = await_bank(act, bank + k)
                        nc.scalar.activation(mixT1[:, 4 * k:4 * k + 4, :], halves(w, 4), ACT.Copy)\
                            .then_inc(free[(bank + k) % WB], 1)
                elif kind == "FINAL":
                    norm(args[0], at.x_writes)

        @block.vector
        def _(dve):
            links = [0]
            seen = {"act": 0, "norm": 0}
            scores_bank = {}

            def link(ins):
                links[0] += 1
                ins.then_inc(dve_link, 1)
                dve.wait_ge(dve_link, links[0])

            def await_act():
                seen["act"] += 1
                dve.wait_ge(act_out, seen["act"])

            def norm(b, g):
                k = seen["norm"]
                seen["norm"] += 1
                dve.wait_ge(sq_ready, k + 1)
                nc.vector.tensor_scalar(roots[:, 0, k:k + 1], squares[:, k:k + 1], 1.0 / D, EPS, ALU.mult, ALU.add)\
                    .then_inc(mean_ready, 1)
                dve.wait_ge(root_ready, k + 1)
                link(nc.vector.reciprocal(scale[:, k:k + 1], roots[:, 1, k:k + 1]))
                dve.wait_ge(gain_in[g % 2], 16 * (g // 2 + 1))
                nc.vector.scalar_tensor_tensor(h[:, b, :], x[:, b, :], scale[:, k:k + 1], gain[:, g % 2, :],
                                               ALU.mult, ALU.mult).then_inc(h_ready, 1)

            def mix0(n0):
                for b in range(NBLK):
                    norm(b, 0)
                for k in range(2):
                    n = n0 + B_K + k
                    w = halves(await_bank(dve, n))
                    for j in range(2):
                        for r in range(2):
                            rows = slice(64 * r, 64 * r + 64)
                            last = nc.vector.tensor_copy(kz[rows, 4 * k + 2 * j + r, :], w[rows, j, :])
                    last.then_inc(free[n % WB], 1)

            def mix0_gla(n0):
                q_raw, k_raw = scT[:, 0].rearrange("p j t -> p (j t)"), scT[:, 1].rearrange("p j t -> p (j t)")
                for dst, n in ((q_raw, n0 + B_GQ), (k_raw, n0 + B_GK)):
                    w = await_bank(dve, n)
                    link(nc.vector.tensor_copy(dst, w[:, :]))
                    dve.sem_inc(free[n % WB], 1)
                dve.wait_ge(consts_in, 16 * 5)
                for b in range(NBLK):
                    n = n0 + B_GG + b
                    await_act()
                    w = work[n % WB]
                    link(nc.vector.tensor_scalar(gg[:, b, :], gg[:, b, :], 1.0, None, ALU.add))
                    link(nc.vector.reciprocal(gg[:, b, :], gg[:, b, :]))
                    link(nc.vector.tensor_tensor(gg[:, b, :], gg[:, b, :], w[:, :], ALU.mult))
                    link(nc.vector.tensor_tensor(gg[:, b, :], gg[:, b, :], gla_gain[:, :], ALU.mult))
                    dve.sem_inc(free[n % WB], 1)
                await_act()
                link(nc.vector.scalar_tensor_tensor(la, za, 0.0, t1, ALU.min, ALU.subtract))
                for j in range(2):
                    last = nc.vector.tensor_tensor_scan(bc[:, j * T:(j + 1) * T], resets[:, :], la[:, j * T:(j + 1) * T],
                                                        0.0, ALU.mult, ALU.add)
                link(last)
                shape = [P, 2 * T // GC, GC]
                bcc = bc.rearrange("p (c t) -> p c t", t=GC)
                nc.vector.tensor_tensor(t1.rearrange("p (c t) -> p c t", t=GC), bcc[:, :, GC - 1:GC].to_broadcast(shape),
                                        bcc, ALU.subtract).then_inc(dve_out, 1)
                await_act()
                for hd in range(GH):
                    j, rows = hd // 2, slice(64 * (hd % 2), 64 * (hd % 2) + 64)
                    nc.vector.scalar_tensor_tensor(qz[rows, hd, :], q_raw[rows, j * T:(j + 1) * T], GDK ** -0.5,
                                                   eb[rows, j * T:(j + 1) * T], ALU.mult, ALU.mult)
                nc.vector.tensor_tensor(kin.rearrange("p j t -> p (j t)"), k_raw, enb, ALU.mult)
                for c in range(3):
                    cols = slice(c * GC, (c + 1) * GC)
                    at = c % 2 * GC
                    last = nc.vector.tensor_tensor(kdz[:, c, :, at:at + GC],
                                                   k_raw.rearrange("p (j t) -> p j t", t=T)[:, :, cols],
                                                   edec.rearrange("p (j t) -> p j t", t=T)[:, :, cols], ALU.mult)
                last.then_inc(gla_in, 1)
                for c in range(3):
                    n = n0 + B_KV + c
                    w = await_bank(dve, n)
                    for j in range(2):
                        for r in range(2):
                            rows = slice(64 * r, 64 * r + 64)
                            new = w[rows, j * T + r * GDV:j * T + (r + 1) * GDV]
                            if c == 0:
                                last = nc.vector.tensor_copy(state[rows, c, j, :], new)
                            else:
                                e = j * T + c * GC + GC - 1
                                last = nc.vector.scalar_tensor_tensor(state[rows, c, j, :], state[rows, c - 1, j, :],
                                                                      eb[rows, e:e + 1], new, ALU.mult, ALU.add)
                    last.then_inc(gla_states, 1)
                    dve.wait_ge(gla_states, c + 1)
                    dve.sem_inc(free[n % WB], 1)
                for b in range(NBLK):
                    n = n0 + B_GS + b
                    w = await_bank(dve, n)
                    link(nc.vector.tensor_scalar(scT[:, b], halves(w, GH), -LOWEST, LOWEST, ALU.min, ALU.max))
                    for hd in range(GH):
                        last = nc.vector.tensor_tensor(scT[:, b, hd, :], scT[:, b, hd, :], chunk_mask[:, :], ALU.mult)
                    link(last)
                    dve.sem_inc(free[n % WB], 1)
                for b in range(NBLK):
                    await_act()
                nc.vector.tensor_scalar(gla_stat[:, 1, :], gla_stat[:, 0, :], 1.0 / GDV, EPS, ALU.mult, ALU.add)\
                    .then_inc(dve_out, 1)
                await_act()
                link(nc.vector.reciprocal(gla_stat[:, 1, :], gla_stat[:, 2, :]))
                for b in range(NBLK):
                    w = work[(n0 + B_GO + b) % WB]
                    for hd in range(GH):
                        cols = slice(hd * GDV, (hd + 1) * GDV)
                        last = nc.vector.scalar_tensor_tensor(og[:, b, cols], w[:, cols],
                                                              gla_stat[:, 1, b * GH + hd:b * GH + hd + 1],
                                                              gg[:, b, cols], ALU.mult, ALU.mult)
                    last.then_inc(free[(n0 + B_GO + b) % WB], 1)

            def stick_log(n, hd):
                dve.wait_ge(soft_ready, hd + 1)
                s = stick[:, 1, hd % 2, :]
                link(nc.vector.scalar_tensor_tensor(s, work[n % WB][:, 0:3 * P], 0.0, stick[:, 0, hd % 2, :], ALU.max, ALU.add))
                dve.sem_inc(free[n % WB], 1)
                nc.vector.tensor_tensor(s, s, before.rearrange("p a b -> p (a b)"), ALU.mult).then_inc(log_ready, 1)

            def stick_mask(n, hd):
                w = await_bank(dve, n)
                if hd >= 2:
                    dve.wait_ge(prob_ready, hd - 1)
                nc.vector.tensor_tensor(stick[:, 2, hd % 2, :], w[:, 0:3 * P],
                                        beyond.rearrange("p a b -> p (a b)"), ALU.add).then_inc(exp_ready, 1)
                dve.wait_ge(exp_ready, hd + 1)
                dve.sem_inc(free[n % WB], 1)

            def top16(values, out_v, out_i, rows):
                for k in range(rows):
                    last = nc.vector.max(out_v[:, k, 0:8], values[:, k, :])
                link(last)
                for k in range(rows):
                    nc.vector.max_index(out_i[:, k, 0:8], out_v[:, k, 0:8], values[:, k, :])
                for k in range(rows):
                    last = nc.vector.match_replace(values[:, k, :], out_v[:, k, 0:8], values[:, k, :], LOWEST)
                link(last)
                for k in range(rows):
                    last = nc.vector.max(out_v[:, k, 8:16], values[:, k, :])
                link(last)
                for k in range(rows):
                    last = nc.vector.max_index(out_i[:, k, 8:16], out_v[:, k, 8:16], values[:, k, :])
                link(last)

            def top_keys(layer, b, scores_bank):
                dve.wait_ge(free[scores_bank % WB], scores_bank // WB + 1)
                top16(score_rows(layer, b).rearrange("p (g n) -> p g n", n=NK), top, topi, 2 * PH)

            def top_pairs(layer, b):
                cand = score_rows(layer, b)
                halves_of = top[:, :, :].rearrange("p (h q) k -> p h q k", q=2)
                shape = [P, PH, TOPK, TOPK]
                link(nc.vector.tensor_tensor(cand.rearrange("p (h a c) -> p h a c", h=PH, a=TOPK),
                                             halves_of[:, :, 0, :].unsqueeze(3).to_broadcast(shape),
                                             halves_of[:, :, 1, :].unsqueeze(2).to_broadcast(shape), ALU.add))
                top16(cand.rearrange("p (h n) -> p h n", h=PH), best, where, PH)

            def expert_ids(layer, b):
                w = where[:, :, :].rearrange("p h k -> p (h k)")
                nc.vector.tensor_scalar(digit[:, 0, :], w, 4, None, ALU.logical_shift_right)
                nc.vector.tensor_scalar(digit[:, 1, :], w, 15, None, ALU.bitwise_and)
                link(nc.vector.tensor_copy(topf[:, :, :], topi[:, :, :]))
                link(nc.vector.tensor_copy(digitf[:, :, :], digit[:, :, :]))
                hot = score_rows(layer, b).rearrange("p (n a) -> p n a", a=TOPK)
                hot4 = score_rows(layer, b).rearrange("p (h k a) -> p h k a", h=PH, a=TOPK)
                keys = topf[:, :, :].rearrange("p (h q) k -> p h q k", q=2)
                for q in range(2):
                    link(nc.vector.tensor_tensor(hot, digitf[:, q, :].unsqueeze(2).to_broadcast([P, NE, TOPK]),
                                                 digits[:, :].unsqueeze(1).to_broadcast([P, NE, TOPK]), ALU.is_equal))
                    link(nc.vector.tensor_tensor(hot4, hot4,
                                                 keys[:, :, q, :].unsqueeze(2).to_broadcast([P, PH, TOPK, TOPK]), ALU.mult))
                    link(nc.vector.tensor_reduce(picked[:, q, :], hot, AX.X, ALU.add))
                link(nc.vector.tensor_scalar(picked[:, 0, :], picked[:, 0, :], float(NK), float(layer * NK * NK),
                                             ALU.mult, ALU.add))
                nc.vector.tensor_tensor(experts[:, b, :], picked[:, 0, :], picked[:, 1, :], ALU.add).then_inc(experts_ready, 1)

            def expert_gates(layer, b):
                g3 = gates[:, b, :].rearrange("p (h k) -> p h k", h=PH)
                shape = [P, PH, TOPK]
                nc.vector.tensor_tensor(g3, best[:, :, :], best[:, :, 0:1].to_broadcast(shape), ALU.subtract)\
                    .then_inc(dve_out, 1)
                await_act()
                link(nc.vector.tensor_reduce(gsum[:, 0, :], g3, AX.X, ALU.add))
                link(nc.vector.reciprocal(gsum[:, 1, :], gsum[:, 0, :]))
                link(nc.vector.tensor_tensor(g3, g3, gsum[:, 1, :].unsqueeze(2).to_broadcast(shape), ALU.mult))

            dve.sem_inc(dots_done, 2)
            dve.wait_ge(masks, N_MASKS)
            for kind, args, at in walk():
                bank, chunk = at.bank, at.chunk
                if kind == "MIX0":
                    mix0(bank)
                    mix0_gla(bank)
                    stick_log(bank + B_Z[0], 0)
                    for hd in range(SBH):
                        if hd + 1 < SBH:
                            stick_log(bank + B_Z[hd + 1], hd + 1)
                        stick_mask(bank + B_E[hd], hd)
                    for n in range(2):
                        for b in range(NBLK):
                            k = bank + B_OUT + 2 * n + b
                            w = await_bank(dve, k)
                            xs = x[:, b, n * CH:(n + 1) * CH]
                            link(nc.vector.tensor_tensor(xs, xs, w[:, :], ALU.add))
                            dve.sem_inc(free[k % WB], 1)
                            if n == 1:
                                dve.sem_inc(x_ready, 1)
                elif kind == "QNORM":
                    for b in args[1]:
                        norm(b, at.gain)
                elif kind == "QSCORE":
                    if args[2] == 3:
                        for k, b in enumerate(args[1]):
                            scores_bank[args[0], b] = bank + 2 * k + 1
                elif kind == "TOPK":
                    layer, b, part = args
                    if part == 0:
                        top_keys(layer, b, scores_bank[layer, b])
                    else:
                        (top_pairs, expert_ids, expert_gates)[part - 1](layer, b)
                elif kind == "GATHER":
                    layer, b, i0, i1 = args
                    t0 = gather_turn(layer, b)
                    with dve.Fori(i0, i1) as i:
                        def weigh(g):
                            part = slice(g * HALF, (g + 1) * HALF)
                            dve.wait_ge(gelu_done, 2 * (t0 + i) + g + 1)
                            nc.vector.tensor_tensor(wts[:, part], gelus[:, part],
                                                    gates[:, b, bass.ds(i * STEPS + g * HALF, HALF)],
                                                    ALU.mult).then_inc(wts_ready, 1)

                        for k in range(STEPS):
                            dve.wait_ge(u_in[k], 16 * (t0 + i + 1))
                            last = nc.vector.tensor_tensor_reduce(
                                out=ring[:, k, :], in0=ring[:, k, :], in1=h[:, b, :], scale=1.0, scalar=0.0,
                                op0=ALU.mult, op1=ALU.add, accum_out=dots[:, k:k + 1])
                            if k % HALF == HALF - 1:
                                last.then_inc(dots_done, 1)
                            if k == HALF:
                                weigh(0)
                        weigh(1)
                elif kind == "ADD":
                    layer, b = args
                    dve.wait_ge(v_used, 2 * (gather_turn(layer, b) + TURNS) + 2)
                    nc.vector.tensor_copy(x[:, b, 0:CH], acc[2 * b][:, :])
                    nc.vector.tensor_copy(x[:, b, CH:D], acc[2 * b + 1][:, :]).then_inc(x_ready, 1)
                elif kind == "ZNORM":
                    norm(args[0], at.gain)
                elif kind == "VNORM":
                    b = args[0]
                    k = VNORM_COL + b
                    await_act()
                    nc.vector.tensor_scalar(roots[:, 0, k:k + 1], squares[:, k:k + 1], 1.0 / SGW, EPS, ALU.mult, ALU.add)\
                        .then_inc(dve_out, 1)
                    await_act()
                    link(nc.vector.reciprocal(scale[:, k:k + 1], roots[:, 1, k:k + 1]))
                    dve.wait_ge(nat_in, 16 * at.nat)
                    nc.vector.scalar_tensor_tensor(z[:, SGW:2 * SGW], z[:, SGW:2 * SGW], scale[:, k:k + 1],
                                                   nat[:, :], ALU.mult, ALU.mult).then_inc(v_ready, 1)
                elif kind == "MIXG":
                    for k in range(4):
                        w = await_bank(dve, bank + k)
                        for g in (2 * k, 2 * k + 1):
                            u = z[:, g * SGC:(g + 1) * SGC]
                            last = nc.vector.scalar_tensor_tensor(u, w[:, g % 2 * SGC:(g % 2 + 1) * SGC],
                                                                  b_spatial[:, g:g + 1], u, ALU.add, ALU.mult)
                        last.then_inc(free[(bank + k) % WB], 1)
                elif kind == "MIXO":
                    b, n = args
                    w = await_bank(dve, bank)
                    xs = x[:, b, n * CH:(n + 1) * CH]
                    link(nc.vector.tensor_tensor(xs, xs, w[:, :], ALU.add))
                    dve.sem_inc(free[bank % WB], 1)
                    if n == 1:
                        dve.sem_inc(x_ready, 1)
                elif kind == "FINAL":
                    norm(args[0], at.gain)

        @block.tensor
        def _(pe):
            seen = {"norm": 0}
            hT_banks = [None]

            def transpose(dst, src):
                return nc.tensor.matmul(dst, src, ident[:, :], is_transpose=True, start=True, stop=True)

            def make_hT(n, b):
                seen["norm"] += 1
                pe.wait_ge(h_ready, seen["norm"])
                for half in range(2):
                    w = claim_bank(pe, n + half)
                    for c in range(4):
                        k = half * 4 + c
                        last = transpose(w[:, c * P:(c + 1) * P], h[:, b, k * P:(k + 1) * P])
                    last.then_inc(full[(n + half) % WB], 1)

            def own_copies(n, count):
                for k in range(n, n + count):
                    pe.wait_ge(free[k % WB], k // WB + 1)

            def wide(n, chunk, cols):
                tiles = CH // P
                width = cols.stop - cols.start
                per = CH // width
                wt = await_chunk(pe, chunk)
                for t in range(tiles):
                    if t % per == 0:
                        w = claim_bank(pe, n + t // per)
                    dst = w[:, t % per * width:(t % per + 1) * width]
                    for k in range(KT):
                        last = nc.tensor.matmul(dst, wt[:, k, t * P:(t + 1) * P], hT[:, k, cols],
                                                start=(k == 0), stop=(k == KT - 1))
                    if t % per == per - 1:
                        last.then_inc(full[(n + t // per) % WB], 1)

            def tall(n, chunk, src, b):
                wt = await_chunk(pe, chunk)
                w = claim_bank(pe, n)
                for k in range(KT):
                    last = nc.tensor.matmul(w[:, :], src[:, k, b * P:(b + 1) * P], wt[:, k, :],
                                            start=(k == 0), stop=(k == KT - 1))
                last.then_inc(full[n % WB], 1)

            def mix0(n0, c0):
                for b in range(NBLK):
                    make_hT(n0 + 2 * b, b)
                own_copies(n0, 4)
                both = slice(0, T)
                wide(n0 + B_Q, c0, both)
                wide(n0 + B_K, c0 + 1, both)
                for b in range(NBLK):
                    tall(n0 + B_V + b, c0 + 2, hT, b)
                wide(n0 + B_GQ, c0 + 3, both)
                for j in range(2):
                    for b in range(NBLK):
                        tall(n0 + B_GV + 2 * j + b, c0 + 4 + j, hT, b)

            def mix0_gla(n0):
                n = n0 + B_RANK
                w = claim_bank(pe, n)
                pe.wait_ge(consts_in, 16 * 5)
                for k in range(KT):
                    last = nc.tensor.matmul(w[0:RANK, 0:T], w_rank[:, k, :], hT[:, k, :], start=(k == 0), stop=(k == KT - 1))
                last.then_inc(full[n % WB], 1)
                own_copies(n, 1)
                n = n0 + B_ALPHA
                w = claim_bank(pe, n)
                for j in range(2):
                    last = nc.tensor.matmul(w[:, j * T:(j + 1) * T], w_alpha[:, j * P:(j + 1) * P], alphaT[:, :],
                                            start=True, stop=True)
                last.then_inc(full[n % WB], 1)
                pe.wait_ge(gla_in, 1)
                for k in range(2):
                    w = claim_bank(pe, n0 + B_KD + k)
                    pairs = [(c, j) for c in ((0, 1) if k == 0 else (2,)) for j in range(2)]
                    for at, (c, j) in enumerate(pairs):
                        last = transpose(w[:, at * P:(at + 1) * P], kdz[:, c, j, :])
                    last.then_inc(full[(n0 + B_KD + k) % WB], 1)
                own_copies(n0 + B_GV, 2)
                own_copies(n0 + B_KD, 2)
                for c in range(3):
                    n = n0 + B_KV + c
                    w = claim_bank(pe, n)
                    for j in range(2):
                        last = nc.tensor.matmul(w[:, j * T:(j + 1) * T], kd[:, c, j, :],
                                                v_g[:, c // 2, j * T:(j + 1) * T], start=True, stop=True)
                    last.then_inc(full[n % WB], 1)
                for b in range(NBLK):
                    n = n0 + B_GS + b
                    w = claim_bank(pe, n)
                    for hd in range(GH):
                        last = nc.tensor.matmul(w[:, hd * P:(hd + 1) * P], kin[:, hd // 2, b * P:(b + 1) * P],
                                                qz[:, hd, b * P:(b + 1) * P], start=True, stop=True)
                    last.then_inc(full[n % WB], 1)
                for b in range(NBLK):
                    n = n0 + B_GO + b
                    own_copies(n0 + B_GS + b, 1)
                    pe.wait_ge(gla_states, 3)
                    w = claim_bank(pe, n)
                    for hd in range(GH):
                        cols = slice(hd * GDV, (hd + 1) * GDV)
                        nc.tensor.matmul(w[:, cols], scT[:, b, hd, :], v_g[:, b, cols], start=True, stop=True)
                        for c in (2 * b, 2 * b + 1):
                            if c:
                                at = c % 2 * GC
                                last = nc.tensor.matmul(w[at:at + GC, cols], qz[:, hd, c * GC:(c + 1) * GC],
                                                        state[:, c - 1, hd // 2, :], start=False, stop=True,
                                                        skip_group_check=True)
                    last.then_inc(full[n % WB], 1)
                for b in range(NBLK):
                    n = n0 + B_GT + b
                    own_copies(n0 + B_GO + b, 1)
                    w = claim_bank(pe, n)
                    for hd in range(GH):
                        last = transpose(w[:, hd * P:(hd + 1) * P], og[:, b, hd * GDV:(hd + 1) * GDV])
                    last.then_inc(full[n % WB], 1)

            def stick_score(n, hd):
                w = claim_bank(pe, n)
                nc.tensor.matmul(w[:, 0:T], kz[:, hd, 0:P], qT[:, hd // 2, :], start=True, stop=True)
                nc.tensor.matmul(w[:, T:T + P], kz[:, hd, P:T], qT[:, hd // 2, P:T], start=True, stop=True)\
                    .then_inc(full[n % WB], 1)

            def stick_exponent(n, hd):
                w = claim_bank(pe, n)
                pe.wait_ge(log_ready, hd + 1)
                s = stick[:, 1, hd % 2, :]
                nc.tensor.matmul(w[:, 0:T], kz[:, hd, 0:P], qT[:, hd // 2, :], start=True, stop=False)
                nc.tensor.matmul(w[:, 0:T], suffix[:, 0, :], s[:, 0:T], start=False, stop=False)
                nc.tensor.matmul(w[:, P:T], suffix[:, 1, :], s[:, T:T + P], start=False, stop=True)
                nc.tensor.matmul(w[:, T:T + P], kz[:, hd, P:T], qT[:, hd // 2, P:T], start=True, stop=False)
                nc.tensor.matmul(w[:, T:T + P], suffix[:, 0, :], s[:, T:T + P], start=False, stop=True)\
                    .then_inc(full[n % WB], 1)

            def stick_heads(n0):
                own_copies(n0 + B_Q, 6)
                stick_score(n0 + B_Z[0], 0)
                for hd in range(SBH):
                    if hd + 1 < SBH:
                        stick_score(n0 + B_Z[hd + 1], hd + 1)
                    stick_exponent(n0 + B_E[hd], hd)
                pe.wait_ge(prob_ready, SBH)
                for k in range(2):
                    n = n0 + B_SO + k
                    w = claim_bank(pe, n)
                    for j in range(2):
                        for r in range(2):
                            hd = 4 * k + 2 * j + r
                            rows, cols = slice(64 * r, 64 * r + 64), slice(hd * SBD, (hd + 1) * SBD)
                            nc.tensor.matmul(w[rows, j * T:(j + 1) * T], v_sb[:, 0, cols], AT[:, hd, 0:T],
                                             start=True, stop=False)
                            last = nc.tensor.matmul(w[rows, j * T + P:(j + 1) * T], v_sb[:, 1, cols], AT[:, hd, T:T + P],
                                                    start=False, stop=True)
                    last.then_inc(full[n % WB], 1)

            pe.sem_inc(v_used, 2)
            pe.wait_ge(masks, N_MASKS)
            for kind, args, at in walk():
                bank, chunk = at.bank, at.chunk
                if kind == "MIX0":
                    mix0(bank, chunk)
                    mix0_gla(bank)
                    stick_heads(bank)
                    own_copies(bank + B_GT, 2)
                    own_copies(bank + B_SO, 2)
                    for n in range(2):
                        for b in range(NBLK):
                            tall(bank + B_OUT + 2 * n + b, chunk + 6 + n, mixT, b)
                elif kind == "SPATIAL":
                    pe.wait_ge(nat_masked, 1)
                    for k in range(2):
                        w = claim_bank(pe, bank + k)
                        for c in range(4):
                            g = 4 * k + c
                            last = transpose(w[:, c * P:(c + 1) * P], nat[:, g * P:(g + 1) * P])
                        last.then_inc(full[(bank + k) % WB], 1)
                elif kind == "QNORM":
                    for k, b in enumerate(args[1]):
                        make_hT(bank + 2 * k, b)
                    hT_banks[0] = (bank, 2 * len(args[1]))
                elif kind == "QKEYS":
                    pe.wait_ge(nat_in, 16 * (at.nat + 1))
                    for k in range(4):
                        w = claim_bank(pe, bank + k)
                        for c in range(4):
                            g = 4 * k + c
                            last = transpose(w[:, c * P:(c + 1) * P], nat[:, g * P:(g + 1) * P])
                        last.then_inc(full[(bank + k) % WB], 1)
                    own_copies(bank, 4)
                    own_copies(*hT_banks[0])
                elif kind == "QSCORE":
                    layer, blocks, m = args
                    for k, b in enumerate(blocks):
                        n = bank + 2 * k
                        wide(n, chunk, slice(b * P, (b + 1) * P))
                        own_copies(n, 1)
                        w = claim_bank(pe, n + 1)
                        for t in range(4):
                            last = nc.tensor.matmul(w[:, t * P:(t + 1) * P], queries[:, n // 2 % 2, t * P:(t + 1) * P],
                                                    keysT[:, 4 * m + t, :], start=True, stop=True)
                        last.then_inc(full[(n + 1) % WB], 1)
                elif kind == "ACC":
                    layer, b = args
                    pe.wait_ge(x_ready, at.x_writes)
                    for n in range(2):
                        nc.tensor.matmul(acc[2 * b + n][:, :], ident[:, :], x[:, b, n * CH:(n + 1) * CH],
                                         start=True, stop=True)
                elif kind == "GATHER":
                    layer, b, i0, i1 = args
                    t0 = gather_turn(layer, b)
                    with pe.Fori(i0, i1) as i:
                        for k in range(STEPS):
                            g = k // HALF
                            if k % HALF == 0:
                                pe.wait_ge(diag_ready, 2 * (t0 + i) + g + 1)
                            pe.wait_ge(v_in[k], 16 * (t0 + i + 1))
                            for n in range(2):
                                last = nc.tensor.matmul(acc[2 * b + n][:, :], diag[:, k, :],
                                                        ring[:, STEPS + k, n * CH:(n + 1) * CH],
                                                        start=False, stop=True, skip_group_check=True)
                            if k % HALF == HALF - 1:
                                last.then_inc(v_used, 1)
                elif kind == "ZNORM":
                    make_hT(bank, args[0])
                    own_copies(bank, 2)
                elif kind == "ZPROJ":
                    tall(bank, chunk, hT, args[0])
                elif kind == "MIXG":
                    pe.wait_ge(v_ready, args[0] + 1)
                    own_copies(bank - 4, 4)
                    for k in range(4):
                        w = claim_bank(pe, bank + k)
                        for g in (2 * k, 2 * k + 1):
                            last = nc.tensor.matmul(w[:, g % 2 * SGC:(g % 2 + 1) * SGC], spatialT[:, g, :],
                                                    z[:, SGW + g * SGC:SGW + (g + 1) * SGC], start=True, stop=True)
                        last.then_inc(full[(bank + k) % WB], 1)
                elif kind == "MIXT":
                    own_copies(bank - 4, 4)
                    for k in range(4):
                        w = claim_bank(pe, bank + k)
                        for c in range(4):
                            last = transpose(w[:, c * P:(c + 1) * P], z[:, (4 * k + c) * P:(4 * k + c + 1) * P])
                        last.then_inc(full[(bank + k) % WB], 1)
                    own_copies(bank, 4)
                elif kind == "MIXO":
                    b, n = args
                    for kh in range(2):
                        wt = await_chunk(pe, chunk + kh)
                        w = claim_bank(pe, bank) if kh == 0 else w
                        for k in range(KT):
                            last = nc.tensor.matmul(w[:, :], mixT1[:, kh * KT + k, :], wt[:, k, :],
                                                    start=(kh + k == 0), stop=(kh == 1 and k == KT - 1))
                        last.then_inc(full[bank % WB] if kh else half_used, 1)


_INS = ["x", "norm_mix", "norm_ffn", "ab_w_in", "ab_w_alpha2", "ab_b_alpha2", "ab_gla_norm", "ab_w_out",
        "c_w_in", "c_v_norm", "c_w_spatial", "c_b_spatial", "c_w_out", "peer_w_q", "peer_subkeys",
        "peer_u", "peer_v", "final_norm"]


def kernel(**inputs):
    import numpy as _np
    import concourse.bacc as _bacc
    from concourse import mybir as _mybir
    from concourse.bass_utils import run_bass_kernel_spmd as _run

    nc = _bacc.Bacc("TRN2", target_bir_lowering=False, num_devices=1)
    arrays, args = {}, []
    for name in _INS:
        a = _np.ascontiguousarray(inputs[name])
        arrays[f"in_{name}"] = a
        args.append(nc.dram_tensor(f"in_{name}", a.shape, _mybir.dt.from_np(a.dtype), kind="ExternalInput").ap())
    out = nc.dram_tensor("out", (1, T, D), _mybir.dt.float32, kind="ExternalOutput").ap()
    trunk(nc, *args, out)
    r = _run(nc, [arrays], core_ids=[0])
    return r.results[0]["out"]
```

```python
import concourse.bass as bass
from concourse import mybir
from collections import namedtuple
from contextlib import ExitStack

P = 128
NBLK = 2
T = P * NBLK
D = 1024
KT = D // P
CH = 512
EPS = 1e-6
SBH, SBD = 8, 64
GH, GDK, GDV, GC = 4, 64, 128, 64
RANK = 16
GATE_NORM = 16.0
SGW, SGG, SGC = 2048, 8, 256
PH, TOPK, NK = 8, 16, 128
NE = PH * TOPK
NEG = -1.0e30
LOWEST = -3.0e38

STEPS = 8
HALF = STEPS // 2
TURNS = NE // STEPS
PARTS = 4
PART_TURNS = TURNS // PARTS
PHEADS = PH // PARTS
PQ = 2 * PHEADS
WB = 4


B_HT, B_Q, B_K, B_V = 0, 4, 6, 8
B_Z, B_E, B_G = [10], [], []
for _hd in range(SBH):
    if _hd + 1 < SBH:
        B_Z.append(B_Z[0] + 3 * _hd + 1)
    B_E.append(max(B_Z[-1], B_G[-1] if B_G else 0) + 1)
    B_G.append(B_E[-1] + 1)
B_RANK, B_ALPHA, B_GQ, B_GK, B_GV, B_GG = *B_G[:5], B_G[6]
B_SO = B_G[-1] + 1
B_KD = B_SO + 2
B_KV = B_KD + 2
B_GS = B_KV + 3
B_GO = B_GS + NBLK
B_GT = B_GO + NBLK
B_OUT = B_GT + NBLK
MIX0_BANKS = B_OUT + 2 * NBLK
N_CONSTS = 5
N_MASKS = 19
VNORM_COL = 14


def banks_of(kind, args):
    return {"MIX0": lambda: MIX0_BANKS, "SPATIAL": lambda: 2, "TRANSPOSE": lambda: 2 * len(args[0]),
            "QKEYS": lambda: 4, "QSCORE": lambda: 2 * len(args[1]),
            "ZPROJ": lambda: 1, "MIXG": lambda: 4, "MIXT": lambda: 4, "MIXO": lambda: 1,
            }.get(kind, lambda: 0)()


def chunks_of(kind):
    return {"MIX0": 8, "QSCORE": 1, "ZPROJ": 1, "MIXO": 2}.get(kind, 0)


def gather_with(layer, b, others):
    assert max(others) < TURNS
    out, at = [("ACC", layer, b)], 0
    for turn in range(TURNS):
        if turn in others or (turn + 1) % PART_TURNS == 0:
            out.append(("GATHER", layer, b, at, turn + 1))
            out += others.get(turn, [])
            at = turn + 1
    return out + [("ADD", layer, b)]


def trunk_for(b):
    return {0: [("ZNORM", b)],
            1: [("TRANSPOSE", (b,)), ("ZPROJ", b, 4)], 2: [("ZPROJ", b, 5)], 3: [("ZPROJ", b, 6)],
            4: [("ZPROJ", b, 7), ("VNORM", b)], 5: [("ZPROJ", b, 0)], 6: [("ZPROJ", b, 1), ("QKEYS", 1)],
            7: [("ZPROJ", b, 2)], 8: [("ZPROJ", b, 3)], 9: [("MIXG", b)], 10: [("MIXT", b), ("MIXO", b, 0)],
            11: [("MIXO", b, 1), ("QNORM", 1, (b,))],
            12: [("TRANSPOSE", (b,)), ("QSCORE", 1, (b,), 0)],
            13: [("TOPK", 1, b, 0), ("QSCORE", 1, (b,), 1)],
            14: [("TOPK", 1, b, 1), ("QSCORE", 1, (b,), 2)],
            15: [("TOPK", 1, b, 2), ("QSCORE", 1, (b,), 3), ("TOPK", 1, b, 3)]}


PLAN = ([("MIX0",), ("SPATIAL",), ("QKEYS", 0), ("QNORM", 0, (0, 1)), ("TRANSPOSE", (0, 1)),
         ("QSCORE", 0, (0, 1), 0), ("TOPK", 0, 0, 0)]
        + gather_with(0, 0, {0: [("QSCORE", 0, (0, 1), 1)], 1: [("TOPK", 0, 0, 1)],
                             2: [("QSCORE", 0, (0, 1), 2)], 3: [("TOPK", 0, 0, 2)],
                             4: [("QSCORE", 0, (0, 1), 3)], 5: [("TOPK", 0, 0, 3)],
                             7: [("TOPK", 0, 1, 0)], 9: [("TOPK", 0, 1, 1)],
                             11: [("TOPK", 0, 1, 2)], 13: [("TOPK", 0, 1, 3)]})
        + gather_with(0, 1, trunk_for(0))
        + gather_with(1, 0, trunk_for(1))
        + gather_with(1, 1, {0: [("FINAL", 0)]}) + [("FINAL", 1)])


Place = namedtuple("Place", "bank chunk x_writes nat gain")


def walk():
    bank = chunk = x_writes = nat = gain = 0
    for kind, *args in PLAN:
        yield kind, args, Place(bank, chunk, x_writes, nat, gain)
        bank += banks_of(kind, args)
        chunk += chunks_of(kind)
        x_writes += NBLK if kind == "MIX0" else kind == "ADD" or (kind == "MIXO" and args[1] == 1)
        nat += kind in ("SPATIAL", "QKEYS", "ZNORM")
        gain += kind in ("MIX0", "QNORM", "ZNORM", "FINAL")



def trunk(nc, x_in, norm_mix, norm_ffn, ab_w_in, ab_w_alpha2, ab_b_alpha2, ab_gla_norm, ab_w_out,
          c_w_in, c_v_norm, c_w_spatial, c_b_spatial, c_w_out,
          peer_w_q, peer_subkeys, peer_u, peer_v, final_norm, out):
    f32, i32, u32 = mybir.dt.float32, mybir.dt.int32, mybir.dt.uint32
    ALU = mybir.AluOpType
    ACT = mybir.ActivationFunctionType
    AX = mybir.AxisListType
    ctx = ExitStack()
    with ctx:
        def sb(name, shape, dt=f32):
            return ctx.enter_context(nc.sbuf_tensor(name, shape, dt))

        def sem(name):
            return ctx.enter_context(nc.semaphore(name))

        x = sb("x", [P, NBLK, D])
        h = sb("h", [P, NBLK, D])
        hT = sb("hT", [P, KT, T])
        mixT = sb("mixT", [P, KT, T])
        weights = sb("weights", [P, 2, KT, CH])
        ring = sb("ring", [P, 2 * STEPS, D])
        z = sb("z", [P, 2 * SGW])
        scores = sb("scores", [P, 2 * PH * NK])
        gain = sb("gain", [P, 2, D])
        nat = sb("nat", [P, 2 * PH * NK])
        keysT = sb("keysT", [P, 2 * PH, NK])
        spatialT = sb("spatialT", [P, SGG, P])
        queries = sb("queries", [P, 2, CH])
        diag = sb("diag", [P, STEPS, P])
        ident = sb("ident", [P, P])
        digits = sb("digits", [P, TOPK])
        b_spatial = sb("b_spatial", [P, SGG])
        b_alpha = sb("b_alpha", [P, 2])
        w_alpha = sb("w_alpha", [RANK, GH * GDK])
        w_rank = sb("w_rank", [P, KT, RANK])
        squares = sb("squares", [P, 16])
        roots = sb("roots", [P, 2, 16])
        scale = sb("scale", [P, 16])
        gla_stat = sb("gla_stat", [P, 3, NBLK * GH])
        alphaT = sb("alphaT", [RANK, T])
        top = sb("top", [P, PQ, TOPK])
        topi = sb("topi", [P, PQ, TOPK], u32)
        topf = sb("topf", [P, PQ, TOPK])
        best = sb("best", [P, PHEADS, TOPK])
        where = sb("where", [P, PHEADS, TOPK], u32)
        digit = sb("digit", [P, 2, PHEADS * TOPK], u32)
        digitf = sb("digitf", [P, 2, PHEADS * TOPK])
        picked = sb("picked", [P, 2, PHEADS * TOPK])
        gsum = sb("gsum", [P, 2, PHEADS])
        experts = sb("experts", [P, NBLK, NE], i32)
        gates = sb("gates", [P, NBLK, NE])
        idx = sb("idx", [P, 2, STEPS], i32)
        dots = sb("dots", [P, STEPS])
        gelus = sb("gelus", [P, STEPS])
        wts = sb("wts", [P, STEPS])

        acc = [ctx.enter_context(nc.psum_tensor(f"acc{k}", [P, CH], f32)) for k in range(4)]
        work = [ctx.enter_context(nc.psum_tensor(f"work{k}", [P, CH], f32)) for k in range(WB)]

        def slots(k, n=1):
            return ring[:, k:k + n, :].rearrange("p a b -> p (a b)")

        suffix = slots(9)[:, 768:768 + 2 * P].rearrange("p (a b) -> p a b", a=2)
        before = slots(8)[:, 512:512 + 3 * P].rearrange("p (a b) -> p a b", a=3)
        beyond = queries[:, 0, 0:3 * P].rearrange("p (a b) -> p a b", a=3)
        chunk_mask = slots(8)[:, 896:896 + P]
        resets = slots(10)[:, 768:768 + T]
        gla_gain = queries[:, 1, :]
        qT = slots(0).rearrange("p (j t) -> p j t", t=T)
        kz = slots(1, 2).rearrange("p (j t) -> p j t", t=T)
        v_sb = slots(3).rearrange("p (b n) -> p b n", b=NBLK)
        AT = slots(4, 3).rearrange("p (j t) -> p j t", t=3 * P)
        qz = slots(7).rearrange("p (j t) -> p j t", t=T)
        kin = slots(8)[:, 0:2 * T].rearrange("p (j t) -> p j t", t=T)
        kdz = slots(9)[:, 0:768].rearrange("p (c j t) -> p c j t", c=3, j=2)
        kd = slots(10)[:, 0:768].rearrange("p (c j t) -> p c j t", c=3, j=2)
        state = slots(11)[:, 0:768].rearrange("p (c j t) -> p c j t", c=3, j=2)
        v_g = slots(12).rearrange("p (b n) -> p b n", b=NBLK)
        gg = slots(13).rearrange("p (b n) -> p b n", b=NBLK)
        og = slots(14).rearrange("p (b n) -> p b n", b=NBLK)
        scT = slots(15).rearrange("p (b j t) -> p b j t", b=NBLK, j=GH)
        za, t1, la, bc = (scores[:, k * CH:(k + 1) * CH] for k in range(4))
        eb, enb, edec = (z[:, k * CH:(k + 1) * CH] for k in range(3))
        stick = z[:, 1536:1536 + 6 * 384].rearrange("p (k s t) -> p k s t", k=3, s=2)
        mixT1 = mixT[:, :, :].rearrange("p a b -> p (a b)").rearrange("p (k t) -> p k t", t=P)

        full = [sem(f"bank_full{k}") for k in range(WB)]
        free = [sem(f"bank_free{k}") for k in range(WB)]
        chunk_in = [sem(f"chunk_in{k}") for k in range(2)]
        half_used = sem("half_used")
        x_in_sem = sem("x_in")
        consts_in = sem("consts_in")
        gain_in = [sem(f"gain_in{k}") for k in range(2)]
        nat_in = sem("nat_in")
        masks = sem("masks")
        nat_masked = sem("nat_masked")
        x_ready = sem("x_ready")
        sq_ready = sem("sq_ready")
        mean_ready = sem("mean_ready")
        root_ready = sem("root_ready")
        h_ready = sem("h_ready")
        act_link = sem("act_link")
        dve_link = sem("dve_link")
        act_out = sem("act_out")
        dve_out = sem("dve_out")
        experts_ready = sem("experts_ready")
        gates_ready = sem("gates_ready")
        gla_in = sem("gla_in")
        gla_states = sem("gla_states")
        soft_ready = sem("soft_ready")
        log_ready = sem("log_ready")
        exp_ready = sem("exp_ready")
        prob_ready = sem("prob_ready")
        v_ready = sem("v_ready")
        u_in = [sem(f"u_in{k}") for k in range(STEPS)]
        v_in = [sem(f"v_in{k}") for k in range(STEPS)]
        dots_done = sem("dots_done")
        v_used = sem("v_used")
        gelu_done = sem("gelu_done")
        wts_ready = sem("wts_ready")
        diag_ready = sem("diag_ready")
        idx_copied = sem("idx_copied")
        pool_turn = sem("pool_turn")
        stored = sem("stored")

        def await_bank(eng, n):
            eng.wait_ge(full[n % WB], n // WB + 1)
            return work[n % WB]

        def claim_bank(eng, n):
            if n >= WB:
                eng.wait_ge(free[n % WB], n // WB)
            return work[n % WB]

        def await_chunk(eng, n):
            eng.wait_ge(chunk_in[n % 2], 16 * (n // 2 + 1))
            return weights[:, n % 2]

        def gather_turn(layer, b):
            return (2 * layer + b) * TURNS

        def score_rows(layer, b):
            return z[:, 0:2 * PH * NK] if (layer, b) == (0, 1) else scores[:, :]

        def part_of(tile, b, m):
            return tile[:, b, m * PHEADS * TOPK:(m + 1) * PHEADS * TOPK]

        def halves(bank, n=2):
            return bank[:, :].rearrange("p (j t) -> p j t", j=n)

        u_rows = peer_u.rearrange("l e d -> (l e) d")
        v_rows = peer_v.rearrange("l e d -> (l e) d")

        block = ctx.enter_context(nc.Block())

        @block.sync
        def _(sp):
            def tiled(w, r0, c0, cols=CH):
                return w[r0:r0 + D, c0:c0 + cols].rearrange("(k p) n -> p k n", p=P)

            norms = [0]
            chunk_free = []
            nat_free = [None]

            def filled(n):
                return full[n % WB], n // WB + 1

            def load_chunk(n, src, used):
                if n >= 2:
                    sp.wait_ge(*chunk_free[n - 2])
                sp.dma_start(weights[:, n % 2, :, :], src).then_inc(chunk_in[n % 2], 16)
                chunk_free.append(used)

            def load_gain(g, src, n):
                if g >= 2:
                    sp.wait_ge(h_ready, norms[g - 1])
                sp.dma_start(gain[:, g % 2, :], src.partition_broadcast(P)).then_inc(gain_in[g % 2], 16)
                norms.append(norms[-1] + n)

            def load_nat(dst, src, used):
                if nat_free[0]:
                    sp.wait_ge(*nat_free[0])
                sp.dma_start(dst, src).then_inc(nat_in, 16)
                nat_free[0] = used

            halves_used = v_norms = 0
            sp.dma_start(w_rank[:, :, :], tiled(ab_w_in[0], 0, 6 * CH, RANK)).then_inc(consts_in, 16)
            for kind, args, at in walk():
                bank, chunk = at.bank, at.chunk
                if kind == "MIX0":
                    load_gain(at.gain, norm_mix[0], NBLK)
                    for j, last in enumerate((B_Q + 1, B_K + 1, B_V + 1, B_GK, B_G[5], B_G[7])):
                        load_chunk(chunk + j, tiled(ab_w_in[0], 0, j * CH), filled(bank + last))
                    for n in range(2):
                        load_chunk(chunk + 6 + n, tiled(ab_w_out[0], 0, n * CH), filled(bank + B_OUT + 2 * n + 1))
                elif kind == "SPATIAL":
                    load_nat(nat[:, 0:SGG * P].rearrange("t (g s) -> t g s", g=SGG),
                             c_w_spatial[0].rearrange("g t s -> t g s"), filled(bank + 1))
                elif kind == "QNORM":
                    load_gain(at.gain, norm_ffn[args[0]], len(args[1]))
                elif kind == "QKEYS":
                    load_nat(nat[:, :].rearrange("n (g d) -> n g d", d=NK),
                             peer_subkeys[args[0]].rearrange("h q n d -> n (h q) d"), filled(bank + 3))
                elif kind == "QSCORE":
                    load_chunk(chunk, tiled(peer_w_q[args[0]], 0, args[2] * CH), filled(bank + 2 * len(args[1]) - 2))
                elif kind == "ZNORM":
                    v_norms += 1
                    load_gain(at.gain, norm_mix[1], 1)
                    load_nat(nat[:, :], c_v_norm[0].partition_broadcast(P), (v_ready, v_norms))
                elif kind == "ZPROJ":
                    load_chunk(chunk, tiled(c_w_in[0], 0, args[1] * CH), filled(bank))
                elif kind == "MIXO":
                    halves_used += 1
                    for kh in range(2):
                        load_chunk(chunk + kh, tiled(c_w_out[0], kh * D, args[1] * CH),
                                   filled(bank) if kh else (half_used, halves_used))
                elif kind == "FINAL":
                    load_gain(at.gain, final_norm, 1)
                    sp.wait_ge(h_ready, norms[-1])
                    sp.dma_start(out[0, args[0] * P:(args[0] + 1) * P, :], h[:, args[0], :]).then_inc(stored, 16)
            sp.wait_ge(stored, 16 * NBLK)

        @block.gpsimd
        def _(pool):
            step = [0]

            def after(ins):
                step[0] += 1
                ins.then_inc(masks, 1)

            for tile, value in ((ident[:, :], 0.0), (suffix, -1.0), (before, 1.0), (beyond, 0.0), (chunk_mask, 1.0),
                                (resets, 1.0)):
                after(pool.memset(tile, value))
            for tile in (kz, qz, kdz):
                after(pool.memset(tile, 0.0))
            pool.wait_ge(masks, step[0])
            after(pool.affine_select(out=ident[:, :], in_=ident[:, :], compare_op=ALU.not_equal, fill=1.0,
                                     base=0, pattern=[[-1, P]], channel_multiplier=1))
            after(pool.affine_select(out=suffix[:, 0, :], in_=suffix[:, 0, :], compare_op=ALU.is_ge, fill=0.0,
                                     base=0, pattern=[[-1, P]], channel_multiplier=1))
            for part in (0, 2):
                after(pool.affine_select(out=before[:, part, :], in_=before[:, part, :], compare_op=ALU.is_gt,
                                         fill=0.0, base=0, pattern=[[1, P]], channel_multiplier=-1))
                after(pool.affine_select(out=beyond[:, part, :], in_=beyond[:, part, :], compare_op=ALU.is_gt,
                                         fill=NEG, base=0, pattern=[[1, P]], channel_multiplier=-1))
            after(pool.affine_select(out=chunk_mask[:, :], in_=chunk_mask[:, :], compare_op=ALU.is_ge,
                                     fill=0.0, base=0, pattern=[[1, P]], channel_multiplier=-1))
            after(pool.affine_select(out=resets[:, :].rearrange("p (c t) -> p c t", t=GC),
                                     in_=resets[:, :].rearrange("p (c t) -> p c t", t=GC),
                                     compare_op=ALU.not_equal, fill=0.0, base=0,
                                     pattern=[[0, T // GC], [1, GC]], channel_multiplier=0))
            after(pool.iota(digits[:, :], pattern=[[1, TOPK]], base=0, channel_multiplier=0,
                            allow_small_or_imprecise_dtypes=True))
            pool.wait_ge(masks, step[0])
            after(pool.memset(chunk_mask[0:GC, GC:P], 0.0))
            assert step[0] == N_MASKS

            for kind, args, at in walk():
                bank, chunk = at.bank, at.chunk
                if kind == "SPATIAL":
                    pool.wait_ge(nat_in, 16)
                    m = nat[:, 0:SGG * P].rearrange("t (g s) -> t g s", g=SGG)
                    pool.affine_select(out=m, in_=m, compare_op=ALU.is_ge, fill=0.0, base=0,
                                       pattern=[[0, SGG], [-1, P]], channel_multiplier=1).then_inc(nat_masked, 1)
                elif kind == "GATHER":
                    layer, b, i0, i1 = args
                    t0 = gather_turn(layer, b)
                    pool.wait_ge(experts_ready, PARTS * (2 * layer + b) + i0 // PART_TURNS + 1)
                    with pool.Fori(i0, i1) as i:
                        for g in range(2):
                            now = 2 * (t0 + i) + g + 1
                            for t, (table, used, landed) in enumerate(((u_rows, dots_done, u_in), (v_rows, v_used, v_in))):
                                pool.wait_ge(used, now)
                                pool.sem_inc(pool_turn, 1)
                                pool.tensor_copy(idx[:, t, g * HALF:(g + 1) * HALF],
                                                 experts[:, b, bass.ds(i * STEPS + g * HALF, HALF)]).then_inc(idx_copied, 1)
                                pool.wait_ge(idx_copied, 2 * now - 1 + t)
                                pool.sem_inc(pool_turn, 1)
                                for k in range(g * HALF, (g + 1) * HALF):
                                    pool.indirect_dma_start(
                                        ring[:, t * STEPS + k, :], None, table,
                                        bass.IndirectOffsetOnAxis(ap=idx[:, t, k:k + 1], axis=0)).then_inc(landed[k], 16)

        @block.scalar
        def _(act):
            links = [0]
            seen = {"dve": 0, "norm": 0}

            def link(ins):
                links[0] += 1
                ins.then_inc(act_link, 1)
                act.wait_ge(act_link, links[0])

            def await_dve():
                seen["dve"] += 1
                act.wait_ge(dve_out, seen["dve"])

            def norm(b, x_writes):
                k = seen["norm"]
                seen["norm"] += 1
                if k < NBLK:
                    act.wait_ge(x_in_sem, 16)
                else:
                    act.wait_ge(x_ready, x_writes)
                nc.scalar.activation(h[:, b, :], x[:, b, :], ACT.Square,
                                     accum_out=squares[:, k:k + 1]).then_inc(sq_ready, 1)
                act.wait_ge(mean_ready, k + 1)
                nc.scalar.activation(roots[:, 1, k:k + 1], roots[:, 0, k:k + 1], ACT.Sqrt).then_inc(root_ready, 1)

            def take_hT(n, b):
                for half in range(2):
                    w = await_bank(act, n + half)
                    nc.scalar.activation(hT[:, half * 4:half * 4 + 4, b * P:(b + 1) * P], halves(w, 4), ACT.Copy)\
                        .then_inc(free[(n + half) % WB], 1)

            act.dma_start(x[:, :, :], x_in[0].rearrange("(b p) d -> p b d", p=P)).then_inc(x_in_sem, 16)
            act.dma_start(w_alpha[:, :], ab_w_alpha2[0]).then_inc(consts_in, 16)
            act.dma_start(b_alpha[:, :], ab_b_alpha2[0].rearrange("(j p) -> p j", p=P),
                          allow_slow_non_contiguous=True).then_inc(consts_in, 16)
            act.dma_start(gla_gain[:, :], ab_gla_norm[0].partition_broadcast(P)).then_inc(consts_in, 16)
            act.dma_start(b_spatial[:, :], c_b_spatial[0].rearrange("g t -> t g"),
                          allow_slow_non_contiguous=True).then_inc(consts_in, 16)

            def mix0(n0):
                for b in range(NBLK):
                    norm(b, 0)
                for b in range(NBLK):
                    take_hT(n0 + 2 * b, b)
                for j in range(2):
                    n = n0 + B_Q + j
                    w = await_bank(act, n)
                    nc.scalar.activation(qT[:, 2 * j:2 * j + 2, :], halves(w), ACT.Copy, scale=SBD ** -0.5)\
                        .then_inc(free[n % WB], 1)
                for b in range(NBLK):
                    n = n0 + B_V + b
                    w = await_bank(act, n)
                    nc.scalar.activation(v_sb[:, b, :], w[:, :], ACT.Copy).then_inc(free[n % WB], 1)
                stick_soft(n0 + B_Z[0], 0)
                for hd in range(SBH):
                    if hd + 1 < SBH:
                        stick_soft(n0 + B_Z[hd + 1], hd + 1)
                    stick_prob(hd)
                    gla_piece(n0, n0 + B_G[hd])

            def gla_piece(n0, n):
                if n == n0 + B_RANK:
                    w = await_bank(act, n)
                    nc.scalar.activation(alphaT[:, :], w[0:RANK, 0:T], ACT.Copy).then_inc(free[n % WB], 1)
                elif n == n0 + B_ALPHA:
                    w = await_bank(act, n)
                    act.wait_ge(consts_in, 16 * N_CONSTS)
                    for j in range(2):
                        last = nc.scalar.activation(za[:, j * T:(j + 1) * T], w[:, j * T:(j + 1) * T], ACT.Identity,
                                                    bias=b_alpha[:, j:j + 1])
                    link(last)
                    act.sem_inc(free[n % WB], 1)
                    link(nc.scalar.activation(t1, za, ACT.Abs))
                    link(nc.scalar.activation(t1, t1, ACT.Exp, scale=-1.0))
                    nc.scalar.activation(t1, t1, ACT.Ln, bias=1.0).then_inc(act_out, 1)
                elif n == n0 + B_GQ:
                    await_dve()
                    nc.scalar.activation(eb, bc, ACT.Exp, scale=1.0 / GATE_NORM)
                    nc.scalar.activation(enb, bc, ACT.Exp, scale=-1.0 / GATE_NORM)
                    nc.scalar.activation(edec, t1, ACT.Exp, scale=1.0 / GATE_NORM).then_inc(act_out, 1)
                elif n in (n0 + B_GV, n0 + B_GV + 3):
                    w = await_bank(act, n)
                    nc.scalar.activation(v_g[:, int(n != n0 + B_GV), :], w[:, :], ACT.Copy).then_inc(free[n % WB], 1)
                elif n in (n0 + B_G[6], n0 + B_G[7]):
                    w = await_bank(act, n)
                    nc.scalar.activation(gg[:, int(n == n0 + B_G[7]), :], w[:, :], ACT.Exp, scale=-1.0).then_inc(act_out, 1)

            def mix0_gla(n0):
                for k in range(2):
                    w = await_bank(act, n0 + B_KD + k)
                    n = 4 if k == 0 else 2
                    dst = kd[:, 2 * k:2 * k + n // 2].rearrange("p c j t -> p (c j t)")
                    nc.scalar.activation(dst, w[:, 0:n * P], ACT.Copy).then_inc(free[(n0 + B_KD + k) % WB], 1)
                for b in range(NBLK):
                    w = await_bank(act, n0 + B_GO + b)
                    for hd in range(GH):
                        last = nc.scalar.activation(og[:, b, hd * GDV:(hd + 1) * GDV], w[:, hd * GDV:(hd + 1) * GDV],
                                                    ACT.Square, accum_out=gla_stat[:, 0, b * GH + hd:b * GH + hd + 1])
                    last.then_inc(act_out, 1)
                await_dve()
                nc.scalar.activation(gla_stat[:, 2, :], gla_stat[:, 1, :], ACT.Sqrt).then_inc(act_out, 1)
                for b in range(NBLK):
                    w = await_bank(act, n0 + B_GT + b)
                    nc.scalar.activation(mixT[:, 4:8, b * P:(b + 1) * P], halves(w, 4), ACT.Copy)\
                        .then_inc(free[(n0 + B_GT + b) % WB], 1)

            def stick_soft(n, hd):
                w = await_bank(act, n)
                s = stick[:, 0, hd % 2, :]
                if hd >= 2:
                    act.wait_ge(log_ready, hd - 1)
                link(nc.scalar.activation(s, w[:, 0:3 * P], ACT.Abs))
                link(nc.scalar.activation(s, s, ACT.Exp, scale=-1.0))
                nc.scalar.activation(s, s, ACT.Ln, bias=1.0).then_inc(soft_ready, 1)

            def stick_prob(hd):
                act.wait_ge(exp_ready, hd + 1)
                nc.scalar.activation(AT[:, hd, :], stick[:, 2, hd % 2, :], ACT.Exp).then_inc(prob_ready, 1)

            for kind, args, at in walk():
                bank, chunk = at.bank, at.chunk
                if kind == "MIX0":
                    mix0(bank)
                    for k in range(2):
                        n = bank + B_SO + k
                        w = await_bank(act, n)
                        nc.scalar.activation(mixT[:, 2 * k:2 * k + 2, :], halves(w), ACT.Copy).then_inc(free[n % WB], 1)
                    mix0_gla(bank)
                elif kind == "SPATIAL":
                    for k in range(2):
                        w = await_bank(act, bank + k)
                        nc.scalar.activation(spatialT[:, 4 * k:4 * k + 4, :], halves(w, 4), ACT.Copy)\
                            .then_inc(free[(bank + k) % WB], 1)
                elif kind == "QNORM":
                    for b in args[1]:
                        norm(b, at.x_writes)
                elif kind == "TRANSPOSE":
                    for k, b in enumerate(args[0]):
                        take_hT(bank + 2 * k, b)
                elif kind == "QKEYS":
                    for k in range(4):
                        w = await_bank(act, bank + k)
                        nc.scalar.activation(keysT[:, 4 * k:4 * k + 4, :], halves(w, 4), ACT.Copy)\
                            .then_inc(free[(bank + k) % WB], 1)
                elif kind == "QSCORE":
                    layer, blocks, m = args
                    for k, b in enumerate(blocks):
                        n = bank + 2 * k
                        w = await_bank(act, n)
                        nc.scalar.activation(queries[:, n // 2 % 2, :], w[:, :], ACT.Copy).then_inc(free[n % WB], 1)
                        w = await_bank(act, n + 1)
                        dst = score_rows(layer, b)[:, m * CH:(m + 1) * CH]
                        nc.scalar.activation(dst, w[:, :], ACT.Copy).then_inc(free[(n + 1) % WB], 1)
                elif kind == "TOPK":
                    await_dve()
                    g = part_of(gates, args[1], args[2])
                    nc.scalar.activation(g, g, ACT.Exp).then_inc(act_out, 1)
                elif kind == "GATHER":
                    layer, b, i0, i1 = args
                    t0 = gather_turn(layer, b)
                    with act.Fori(i0, i1) as i:
                        for g in range(2):
                            now = 2 * (t0 + i) + g + 1
                            part = slice(g * HALF, (g + 1) * HALF)
                            act.wait_ge(dots_done, now + 2)
                            nc.scalar.activation(gelus[:, part], dots[:, part], ACT.Gelu).then_inc(gelu_done, 1)
                            act.wait_ge(wts_ready, now)
                            act.wait_ge(v_used, now)
                            for k in range(g * HALF, (g + 1) * HALF):
                                last = nc.scalar.activation(diag[:, k, :], ident[:, :], ACT.Copy, scale=wts[:, k:k + 1])
                            last.then_inc(diag_ready, 1)
                elif kind == "ZNORM":
                    norm(args[0], at.x_writes)
                elif kind == "ZPROJ":
                    w = await_bank(act, bank)
                    cols = slice(args[1] * CH, (args[1] + 1) * CH)
                    nc.scalar.activation(z[:, cols], w[:, :], ACT.Gelu).then_inc(free[bank % WB], 1)
                elif kind == "VNORM":
                    for n in range(bank - 4, bank):
                        act.wait_ge(free[n % WB], n // WB + 1)
                    nc.scalar.activation(mixT[:, :, :].rearrange("p a b -> p (a b)"), z[:, SGW:2 * SGW], ACT.Square,
                                         accum_out=squares[:, VNORM_COL + args[0]:VNORM_COL + args[0] + 1]).then_inc(act_out, 1)
                    await_dve()
                    nc.scalar.activation(roots[:, 1, VNORM_COL + args[0]:VNORM_COL + args[0] + 1], roots[:, 0, VNORM_COL + args[0]:VNORM_COL + args[0] + 1],
                                         ACT.Sqrt).then_inc(act_out, 1)
                elif kind == "MIXT":
                    for k in range(4):
                        w = await_bank(act, bank + k)
                        nc.scalar.activation(mixT1[:, 4 * k:4 * k + 4, :], halves(w, 4), ACT.Copy)\
                            .then_inc(free[(bank + k) % WB], 1)
                elif kind == "FINAL":
                    norm(args[0], at.x_writes)

        @block.vector
        def _(dve):
            links = [0]
            seen = {"act": 0, "norm": 0}
            scores_bank = {}

            def link(ins):
                links[0] += 1
                ins.then_inc(dve_link, 1)
                dve.wait_ge(dve_link, links[0])

            def await_act():
                seen["act"] += 1
                dve.wait_ge(act_out, seen["act"])

            def norm(b, g):
                k = seen["norm"]
                seen["norm"] += 1
                dve.wait_ge(sq_ready, k + 1)
                nc.vector.tensor_scalar(roots[:, 0, k:k + 1], squares[:, k:k + 1], 1.0 / D, EPS, ALU.mult, ALU.add)\
                    .then_inc(mean_ready, 1)
                dve.wait_ge(root_ready, k + 1)
                link(nc.vector.reciprocal(scale[:, k:k + 1], roots[:, 1, k:k + 1]))
                dve.wait_ge(gain_in[g % 2], 16 * (g // 2 + 1))
                nc.vector.scalar_tensor_tensor(h[:, b, :], x[:, b, :], scale[:, k:k + 1], gain[:, g % 2, :],
                                               ALU.mult, ALU.mult).then_inc(h_ready, 1)

            def mix0(n0):
                for b in range(NBLK):
                    norm(b, 0)
                for k in range(2):
                    n = n0 + B_K + k
                    w = halves(await_bank(dve, n))
                    for j in range(2):
                        for r in range(2):
                            rows = slice(64 * r, 64 * r + 64)
                            last = nc.vector.tensor_copy(kz[rows, 4 * k + 2 * j + r, :], w[rows, j, :])
                    last.then_inc(free[n % WB], 1)
                stick_log(n0 + B_Z[0], 0)
                for hd in range(SBH):
                    if hd + 1 < SBH:
                        stick_log(n0 + B_Z[hd + 1], hd + 1)
                    stick_mask(n0 + B_E[hd], hd)
                    gla_piece(n0, n0 + B_G[hd])

            q_raw, k_raw = scT[:, 0].rearrange("p j t -> p (j t)"), scT[:, 1].rearrange("p j t -> p (j t)")

            def gla_piece(n0, n):
                if n == n0 + B_ALPHA:
                    await_act()
                    link(nc.vector.scalar_tensor_tensor(la, za, 0.0, t1, ALU.min, ALU.subtract))
                    for j in range(2):
                        last = nc.vector.tensor_tensor_scan(bc[:, j * T:(j + 1) * T], resets[:, :], la[:, j * T:(j + 1) * T],
                                                            0.0, ALU.mult, ALU.add)
                    link(last)
                    shape = [P, 2 * T // GC, GC]
                    bcc = bc.rearrange("p (c t) -> p c t", t=GC)
                    nc.vector.tensor_tensor(t1.rearrange("p (c t) -> p c t", t=GC), bcc[:, :, GC - 1:GC].to_broadcast(shape),
                                            bcc, ALU.subtract).then_inc(dve_out, 1)
                elif n == n0 + B_GQ:
                    w = await_bank(dve, n)
                    link(nc.vector.tensor_copy(q_raw, w[:, :]))
                    dve.sem_inc(free[n % WB], 1)
                elif n == n0 + B_GK:
                    w = await_bank(dve, n)
                    link(nc.vector.tensor_copy(k_raw, w[:, :]))
                    dve.sem_inc(free[n % WB], 1)
                    gla_gated()
                elif n in (n0 + B_G[6], n0 + B_G[7]):
                    dve.wait_ge(consts_in, 16 * N_CONSTS)
                    await_act()
                    g, w = gg[:, int(n == n0 + B_G[7]), :], work[n % WB]
                    link(nc.vector.tensor_scalar(g, g, 1.0, None, ALU.add))
                    link(nc.vector.reciprocal(g, g))
                    link(nc.vector.tensor_tensor(g, g, w[:, :], ALU.mult))
                    link(nc.vector.tensor_tensor(g, g, gla_gain, ALU.mult))
                    dve.sem_inc(free[n % WB], 1)

            def gla_gated():
                await_act()
                for hd in range(GH):
                    j, rows = hd // 2, slice(64 * (hd % 2), 64 * (hd % 2) + 64)
                    nc.vector.scalar_tensor_tensor(qz[rows, hd, :], q_raw[rows, j * T:(j + 1) * T], GDK ** -0.5,
                                                   eb[rows, j * T:(j + 1) * T], ALU.mult, ALU.mult)
                nc.vector.tensor_tensor(kin.rearrange("p j t -> p (j t)"), k_raw, enb, ALU.mult)
                for c in range(3):
                    cols = slice(c * GC, (c + 1) * GC)
                    at = c % 2 * GC
                    last = nc.vector.tensor_tensor(kdz[:, c, :, at:at + GC],
                                                   k_raw.rearrange("p (j t) -> p j t", t=T)[:, :, cols],
                                                   edec.rearrange("p (j t) -> p j t", t=T)[:, :, cols], ALU.mult)
                last.then_inc(gla_in, 1)

            def mix0_gla(n0):
                for c in range(3):
                    n = n0 + B_KV + c
                    w = await_bank(dve, n)
                    for j in range(2):
                        for r in range(2):
                            rows = slice(64 * r, 64 * r + 64)
                            new = w[rows, j * T + r * GDV:j * T + (r + 1) * GDV]
                            if c == 0:
                                last = nc.vector.tensor_copy(state[rows, c, j, :], new)
                            else:
                                e = j * T + c * GC + GC - 1
                                last = nc.vector.scalar_tensor_tensor(state[rows, c, j, :], state[rows, c - 1, j, :],
                                                                      eb[rows, e:e + 1], new, ALU.mult, ALU.add)
                    last.then_inc(gla_states, 1)
                    dve.wait_ge(gla_states, c + 1)
                    dve.sem_inc(free[n % WB], 1)
                for b in range(NBLK):
                    n = n0 + B_GS + b
                    w = await_bank(dve, n)
                    link(nc.vector.tensor_scalar(scT[:, b], halves(w, GH), -LOWEST, LOWEST, ALU.min, ALU.max))
                    for hd in range(GH):
                        last = nc.vector.tensor_tensor(scT[:, b, hd, :], scT[:, b, hd, :], chunk_mask[:, :], ALU.mult)
                    link(last)
                    dve.sem_inc(free[n % WB], 1)
                for b in range(NBLK):
                    await_act()
                nc.vector.tensor_scalar(gla_stat[:, 1, :], gla_stat[:, 0, :], 1.0 / GDV, EPS, ALU.mult, ALU.add)\
                    .then_inc(dve_out, 1)
                await_act()
                link(nc.vector.reciprocal(gla_stat[:, 1, :], gla_stat[:, 2, :]))
                for b in range(NBLK):
                    w = work[(n0 + B_GO + b) % WB]
                    for hd in range(GH):
                        cols = slice(hd * GDV, (hd + 1) * GDV)
                        last = nc.vector.scalar_tensor_tensor(og[:, b, cols], w[:, cols],
                                                              gla_stat[:, 1, b * GH + hd:b * GH + hd + 1],
                                                              gg[:, b, cols], ALU.mult, ALU.mult)
                    last.then_inc(free[(n0 + B_GO + b) % WB], 1)

            def stick_log(n, hd):
                dve.wait_ge(soft_ready, hd + 1)
                s = stick[:, 1, hd % 2, :]
                link(nc.vector.scalar_tensor_tensor(s, work[n % WB][:, 0:3 * P], 0.0, stick[:, 0, hd % 2, :], ALU.max, ALU.add))
                dve.sem_inc(free[n % WB], 1)
                nc.vector.tensor_tensor(s, s, before.rearrange("p a b -> p (a b)"), ALU.mult).then_inc(log_ready, 1)

            def stick_mask(n, hd):
                w = await_bank(dve, n)
                if hd >= 2:
                    dve.wait_ge(prob_ready, hd - 1)
                nc.vector.tensor_tensor(stick[:, 2, hd % 2, :], w[:, 0:3 * P],
                                        beyond.rearrange("p a b -> p (a b)"), ALU.add).then_inc(exp_ready, 1)
                dve.wait_ge(exp_ready, hd + 1)
                dve.sem_inc(free[n % WB], 1)

            def top16(values, out_v, out_i, rows):
                for k in range(rows):
                    last = nc.vector.max(out_v[:, k, 0:8], values[:, k, :])
                link(last)
                for k in range(rows):
                    nc.vector.max_index(out_i[:, k, 0:8], out_v[:, k, 0:8], values[:, k, :])
                for k in range(rows):
                    last = nc.vector.match_replace(values[:, k, :], out_v[:, k, 0:8], values[:, k, :], LOWEST)
                link(last)
                for k in range(rows):
                    last = nc.vector.max(out_v[:, k, 8:16], values[:, k, :])
                link(last)
                for k in range(rows):
                    last = nc.vector.max_index(out_i[:, k, 8:16], out_v[:, k, 8:16], values[:, k, :])
                link(last)

            def top_keys(rows, n):
                dve.wait_ge(free[n % WB], n // WB + 1)
                top16(rows.rearrange("p (g n) -> p g n", n=NK), top, topi, PQ)

            def top_pairs(rows):
                pair = top[:, :, :].rearrange("p (h q) k -> p h q k", q=2)
                shape = [P, PHEADS, TOPK, TOPK]
                link(nc.vector.tensor_tensor(rows.rearrange("p (h a c) -> p h a c", h=PHEADS, a=TOPK),
                                             pair[:, :, 0, :].unsqueeze(3).to_broadcast(shape),
                                             pair[:, :, 1, :].unsqueeze(2).to_broadcast(shape), ALU.add))
                top16(rows.rearrange("p (h n) -> p h n", h=PHEADS), best, where, PHEADS)

            def expert_ids(layer, b, m, rows):
                w = where[:, :, :].rearrange("p h k -> p (h k)")
                nc.vector.tensor_scalar(digit[:, 0, :], w, 4, None, ALU.logical_shift_right)
                nc.vector.tensor_scalar(digit[:, 1, :], w, 15, None, ALU.bitwise_and)
                link(nc.vector.tensor_copy(topf[:, :, :], topi[:, :, :]))
                link(nc.vector.tensor_copy(digitf[:, :, :], digit[:, :, :]))
                n = PHEADS * TOPK
                hot = rows.rearrange("p (n a) -> p n a", a=TOPK)
                hot4 = rows.rearrange("p (h k a) -> p h k a", h=PHEADS, a=TOPK)
                keys = topf[:, :, :].rearrange("p (h q) k -> p h q k", q=2)
                for q in range(2):
                    link(nc.vector.tensor_tensor(hot, digitf[:, q, :].unsqueeze(2).to_broadcast([P, n, TOPK]),
                                                 digits[:, :].unsqueeze(1).to_broadcast([P, n, TOPK]), ALU.is_equal))
                    link(nc.vector.tensor_tensor(hot4, hot4,
                                                 keys[:, :, q, :].unsqueeze(2).to_broadcast([P, PHEADS, TOPK, TOPK]), ALU.mult))
                    link(nc.vector.tensor_reduce(picked[:, q, :], hot, AX.X, ALU.add))
                link(nc.vector.tensor_scalar(picked[:, 0, :], picked[:, 0, :], float(NK), float(layer * NK * NK),
                                             ALU.mult, ALU.add))
                nc.vector.tensor_tensor(part_of(experts, b, m), picked[:, 0, :], picked[:, 1, :], ALU.add)\
                    .then_inc(experts_ready, 1)

            def gate_shift(b, m):
                g3 = part_of(gates, b, m).rearrange("p (h k) -> p h k", h=PHEADS)
                nc.vector.tensor_tensor(g3, best[:, :, :], best[:, :, 0:1].to_broadcast([P, PHEADS, TOPK]), ALU.subtract)\
                    .then_inc(dve_out, 1)

            def gate_norm(b, m):
                g3 = part_of(gates, b, m).rearrange("p (h k) -> p h k", h=PHEADS)
                await_act()
                link(nc.vector.tensor_reduce(gsum[:, 0, :], g3, AX.X, ALU.add))
                link(nc.vector.reciprocal(gsum[:, 1, :], gsum[:, 0, :]))
                link(nc.vector.tensor_tensor(g3, g3, gsum[:, 1, :].unsqueeze(2).to_broadcast([P, PHEADS, TOPK]), ALU.mult))

            dve.sem_inc(dots_done, 2)
            dve.wait_ge(masks, N_MASKS)
            for kind, args, at in walk():
                bank, chunk = at.bank, at.chunk
                if kind == "MIX0":
                    mix0(bank)
                    mix0_gla(bank)
                    for n in range(2):
                        for b in range(NBLK):
                            k = bank + B_OUT + 2 * n + b
                            w = await_bank(dve, k)
                            xs = x[:, b, n * CH:(n + 1) * CH]
                            link(nc.vector.tensor_tensor(xs, xs, w[:, :], ALU.add))
                            dve.sem_inc(free[k % WB], 1)
                            if n == 1:
                                dve.sem_inc(x_ready, 1)
                elif kind == "QNORM":
                    for b in args[1]:
                        norm(b, at.gain)
                elif kind == "QSCORE":
                    for k, b in enumerate(args[1]):
                        scores_bank[args[0], b, args[2]] = bank + 2 * k + 1
                elif kind == "TOPK":
                    layer, b, m = args
                    rows = score_rows(layer, b)[:, m * CH:(m + 1) * CH]
                    top_keys(rows, scores_bank[layer, b, m])
                    top_pairs(rows)
                    gate_shift(b, m)
                    expert_ids(layer, b, m, rows)
                    gate_norm(b, m)
                elif kind == "GATHER":
                    layer, b, i0, i1 = args
                    t0 = gather_turn(layer, b)
                    with dve.Fori(i0, i1) as i:
                        def weigh(g):
                            part = slice(g * HALF, (g + 1) * HALF)
                            dve.wait_ge(gelu_done, 2 * (t0 + i) + g + 1)
                            nc.vector.tensor_tensor(wts[:, part], gelus[:, part],
                                                    gates[:, b, bass.ds(i * STEPS + g * HALF, HALF)],
                                                    ALU.mult).then_inc(wts_ready, 1)

                        for k in range(STEPS):
                            dve.wait_ge(u_in[k], 16 * (t0 + i + 1))
                            last = nc.vector.tensor_tensor_reduce(
                                out=ring[:, k, :], in0=ring[:, k, :], in1=h[:, b, :], scale=1.0, scalar=0.0,
                                op0=ALU.mult, op1=ALU.add, accum_out=dots[:, k:k + 1])
                            if k % HALF == HALF - 1:
                                last.then_inc(dots_done, 1)
                            if k == HALF:
                                weigh(0)
                        weigh(1)
                elif kind == "ADD":
                    layer, b = args
                    dve.wait_ge(v_used, 2 * (gather_turn(layer, b) + TURNS) + 2)
                    nc.vector.tensor_copy(x[:, b, 0:CH], acc[2 * b][:, :])
                    nc.vector.tensor_copy(x[:, b, CH:D], acc[2 * b + 1][:, :]).then_inc(x_ready, 1)
                elif kind == "ZNORM":
                    norm(args[0], at.gain)
                elif kind == "VNORM":
                    b = args[0]
                    k = VNORM_COL + b
                    await_act()
                    nc.vector.tensor_scalar(roots[:, 0, k:k + 1], squares[:, k:k + 1], 1.0 / SGW, EPS, ALU.mult, ALU.add)\
                        .then_inc(dve_out, 1)
                    await_act()
                    link(nc.vector.reciprocal(scale[:, k:k + 1], roots[:, 1, k:k + 1]))
                    dve.wait_ge(nat_in, 16 * at.nat)
                    nc.vector.scalar_tensor_tensor(z[:, SGW:2 * SGW], z[:, SGW:2 * SGW], scale[:, k:k + 1],
                                                   nat[:, :], ALU.mult, ALU.mult).then_inc(v_ready, 1)
                elif kind == "MIXG":
                    for k in range(4):
                        w = await_bank(dve, bank + k)
                        for g in (2 * k, 2 * k + 1):
                            u = z[:, g * SGC:(g + 1) * SGC]
                            last = nc.vector.scalar_tensor_tensor(u, w[:, g % 2 * SGC:(g % 2 + 1) * SGC],
                                                                  b_spatial[:, g:g + 1], u, ALU.add, ALU.mult)
                        last.then_inc(free[(bank + k) % WB], 1)
                elif kind == "MIXO":
                    b, n = args
                    w = await_bank(dve, bank)
                    xs = x[:, b, n * CH:(n + 1) * CH]
                    link(nc.vector.tensor_tensor(xs, xs, w[:, :], ALU.add))
                    dve.sem_inc(free[bank % WB], 1)
                    if n == 1:
                        dve.sem_inc(x_ready, 1)
                elif kind == "FINAL":
                    norm(args[0], at.gain)

        @block.tensor
        def _(pe):
            seen = {"norm": 0}

            def transpose(dst, src):
                return nc.tensor.matmul(dst, src, ident[:, :], is_transpose=True, start=True, stop=True)

            def make_hT(n, b):
                seen["norm"] += 1
                pe.wait_ge(h_ready, seen["norm"])
                for half in range(2):
                    w = claim_bank(pe, n + half)
                    for c in range(4):
                        k = half * 4 + c
                        last = transpose(w[:, c * P:(c + 1) * P], h[:, b, k * P:(k + 1) * P])
                    last.then_inc(full[(n + half) % WB], 1)

            def own_copies(n, count):
                for k in range(n, n + count):
                    pe.wait_ge(free[k % WB], k // WB + 1)

            def wide(n, chunk, cols, tiles=range(CH // P)):
                width = cols.stop - cols.start
                per = CH // width
                wt = await_chunk(pe, chunk)
                for i, t in enumerate(tiles):
                    if i % per == 0:
                        w = claim_bank(pe, n + i // per)
                    dst = w[:, i % per * width:(i % per + 1) * width]
                    for k in range(KT):
                        last = nc.tensor.matmul(dst, wt[:, k, t * P:(t + 1) * P], hT[:, k, cols],
                                                start=(k == 0), stop=(k == KT - 1))
                    if i % per == per - 1:
                        last.then_inc(full[(n + i // per) % WB], 1)

            def tall(n, chunk, src, b):
                wt = await_chunk(pe, chunk)
                w = claim_bank(pe, n)
                for k in range(KT):
                    last = nc.tensor.matmul(w[:, :], src[:, k, b * P:(b + 1) * P], wt[:, k, :],
                                            start=(k == 0), stop=(k == KT - 1))
                last.then_inc(full[n % WB], 1)

            def mix0(n0, c0):
                for b in range(NBLK):
                    make_hT(n0 + 2 * b, b)
                own_copies(n0, 4)
                both = slice(0, T)
                wide(n0 + B_Q, c0, both)
                wide(n0 + B_K, c0 + 1, both)
                for b in range(NBLK):
                    tall(n0 + B_V + b, c0 + 2, hT, b)
                own_copies(n0 + B_Q, 6)
                stick_score(n0 + B_Z[0], 0)
                for hd in range(SBH):
                    if hd + 1 < SBH:
                        stick_score(n0 + B_Z[hd + 1], hd + 1)
                    stick_exponent(n0 + B_E[hd], hd)
                    n = n0 + B_G[hd]
                    if hd == 0:
                        gate_input(n)
                    elif hd == 1:
                        own_copies(n0 + B_RANK, 1)
                        gate_logits(n)
                    elif hd < 4:
                        wide(n, c0 + 3, both, range(2 * hd - 4, 2 * hd - 2))
                    else:
                        tall(n, c0 + 2 + hd // 2, hT, hd % 2)

            def gate_input(n):
                w = claim_bank(pe, n)
                pe.wait_ge(consts_in, 16 * N_CONSTS)
                for k in range(KT):
                    last = nc.tensor.matmul(w[0:RANK, 0:T], w_rank[:, k, :], hT[:, k, :], start=(k == 0), stop=(k == KT - 1))
                last.then_inc(full[n % WB], 1)

            def gate_logits(n):
                w = claim_bank(pe, n)
                for j in range(2):
                    last = nc.tensor.matmul(w[:, j * T:(j + 1) * T], w_alpha[:, j * P:(j + 1) * P], alphaT[:, :],
                                            start=True, stop=True)
                last.then_inc(full[n % WB], 1)

            def mix0_gla(n0):
                pe.wait_ge(gla_in, 1)
                for k in range(2):
                    w = claim_bank(pe, n0 + B_KD + k)
                    pairs = [(c, j) for c in ((0, 1) if k == 0 else (2,)) for j in range(2)]
                    for at, (c, j) in enumerate(pairs):
                        last = transpose(w[:, at * P:(at + 1) * P], kdz[:, c, j, :])
                    last.then_inc(full[(n0 + B_KD + k) % WB], 1)
                own_copies(n0 + B_GV, 1)
                own_copies(n0 + B_G[5], 1)
                own_copies(n0 + B_KD, 2)
                for c in range(3):
                    n = n0 + B_KV + c
                    w = claim_bank(pe, n)
                    for j in range(2):
                        last = nc.tensor.matmul(w[:, j * T:(j + 1) * T], kd[:, c, j, :],
                                                v_g[:, c // 2, j * T:(j + 1) * T], start=True, stop=True)
                    last.then_inc(full[n % WB], 1)
                for b in range(NBLK):
                    n = n0 + B_GS + b
                    w = claim_bank(pe, n)
                    for hd in range(GH):
                        last = nc.tensor.matmul(w[:, hd * P:(hd + 1) * P], kin[:, hd // 2, b * P:(b + 1) * P],
                                                qz[:, hd, b * P:(b + 1) * P], start=True, stop=True)
                    last.then_inc(full[n % WB], 1)
                for b in range(NBLK):
                    n = n0 + B_GO + b
                    own_copies(n0 + B_GS + b, 1)
                    pe.wait_ge(gla_states, 3)
                    w = claim_bank(pe, n)
                    for hd in range(GH):
                        cols = slice(hd * GDV, (hd + 1) * GDV)
                        nc.tensor.matmul(w[:, cols], scT[:, b, hd, :], v_g[:, b, cols], start=True, stop=True)
                        for c in (2 * b, 2 * b + 1):
                            if c:
                                at = c % 2 * GC
                                last = nc.tensor.matmul(w[at:at + GC, cols], qz[:, hd, c * GC:(c + 1) * GC],
                                                        state[:, c - 1, hd // 2, :], start=False, stop=True,
                                                        skip_group_check=True)
                    last.then_inc(full[n % WB], 1)
                for b in range(NBLK):
                    n = n0 + B_GT + b
                    own_copies(n0 + B_GO + b, 1)
                    w = claim_bank(pe, n)
                    for hd in range(GH):
                        last = transpose(w[:, hd * P:(hd + 1) * P], og[:, b, hd * GDV:(hd + 1) * GDV])
                    last.then_inc(full[n % WB], 1)

            def stick_score(n, hd):
                w = claim_bank(pe, n)
                nc.tensor.matmul(w[:, 0:T], kz[:, hd, 0:P], qT[:, hd // 2, :], start=True, stop=True)
                nc.tensor.matmul(w[:, T:T + P], kz[:, hd, P:T], qT[:, hd // 2, P:T], start=True, stop=True)\
                    .then_inc(full[n % WB], 1)

            def stick_exponent(n, hd):
                w = claim_bank(pe, n)
                pe.wait_ge(log_ready, hd + 1)
                s = stick[:, 1, hd % 2, :]
                nc.tensor.matmul(w[:, 0:T], kz[:, hd, 0:P], qT[:, hd // 2, :], start=True, stop=False)
                nc.tensor.matmul(w[:, 0:T], suffix[:, 0, :], s[:, 0:T], start=False, stop=False)
                nc.tensor.matmul(w[:, P:T], suffix[:, 1, :], s[:, T:T + P], start=False, stop=True)
                nc.tensor.matmul(w[:, T:T + P], kz[:, hd, P:T], qT[:, hd // 2, P:T], start=True, stop=False)
                nc.tensor.matmul(w[:, T:T + P], suffix[:, 0, :], s[:, T:T + P], start=False, stop=True)\
                    .then_inc(full[n % WB], 1)

            def stick_out(n0):
                pe.wait_ge(prob_ready, SBH)
                for k in range(2):
                    n = n0 + B_SO + k
                    w = claim_bank(pe, n)
                    for j in range(2):
                        for r in range(2):
                            hd = 4 * k + 2 * j + r
                            rows, cols = slice(64 * r, 64 * r + 64), slice(hd * SBD, (hd + 1) * SBD)
                            nc.tensor.matmul(w[rows, j * T:(j + 1) * T], v_sb[:, 0, cols], AT[:, hd, 0:T],
                                             start=True, stop=False)
                            last = nc.tensor.matmul(w[rows, j * T + P:(j + 1) * T], v_sb[:, 1, cols], AT[:, hd, T:T + P],
                                                    start=False, stop=True)
                    last.then_inc(full[n % WB], 1)

            pe.sem_inc(v_used, 2)
            pe.wait_ge(masks, N_MASKS)
            for kind, args, at in walk():
                bank, chunk = at.bank, at.chunk
                if kind == "MIX0":
                    mix0(bank, chunk)
                    stick_out(bank)
                    mix0_gla(bank)
                    own_copies(bank + B_GT, 2)
                    own_copies(bank + B_SO, 2)
                    for n in range(2):
                        for b in range(NBLK):
                            tall(bank + B_OUT + 2 * n + b, chunk + 6 + n, mixT, b)
                elif kind == "SPATIAL":
                    pe.wait_ge(nat_masked, 1)
                    for k in range(2):
                        w = claim_bank(pe, bank + k)
                        for c in range(4):
                            g = 4 * k + c
                            last = transpose(w[:, c * P:(c + 1) * P], nat[:, g * P:(g + 1) * P])
                        last.then_inc(full[(bank + k) % WB], 1)
                elif kind == "TRANSPOSE":
                    for k, b in enumerate(args[0]):
                        make_hT(bank + 2 * k, b)
                    own_copies(bank, 2 * len(args[0]))
                elif kind == "QKEYS":
                    pe.wait_ge(nat_in, 16 * (at.nat + 1))
                    for k in range(4):
                        w = claim_bank(pe, bank + k)
                        for c in range(4):
                            g = 4 * k + c
                            last = transpose(w[:, c * P:(c + 1) * P], nat[:, g * P:(g + 1) * P])
                        last.then_inc(full[(bank + k) % WB], 1)
                    own_copies(bank, 4)
                elif kind == "QSCORE":
                    layer, blocks, m = args
                    for k, b in enumerate(blocks):
                        n = bank + 2 * k
                        wide(n, chunk, slice(b * P, (b + 1) * P))
                        own_copies(n, 1)
                        w = claim_bank(pe, n + 1)
                        for t in range(4):
                            last = nc.tensor.matmul(w[:, t * P:(t + 1) * P], queries[:, n // 2 % 2, t * P:(t + 1) * P],
                                                    keysT[:, 4 * m + t, :], start=True, stop=True)
                        last.then_inc(full[(n + 1) % WB], 1)
                elif kind == "ACC":
                    layer, b = args
                    pe.wait_ge(x_ready, at.x_writes)
                    for n in range(2):
                        nc.tensor.matmul(acc[2 * b + n][:, :], ident[:, :], x[:, b, n * CH:(n + 1) * CH],
                                         start=True, stop=True)
                elif kind == "GATHER":
                    layer, b, i0, i1 = args
                    t0 = gather_turn(layer, b)
                    with pe.Fori(i0, i1) as i:
                        for k in range(STEPS):
                            g = k // HALF
                            if k % HALF == 0:
                                pe.wait_ge(diag_ready, 2 * (t0 + i) + g + 1)
                            pe.wait_ge(v_in[k], 16 * (t0 + i + 1))
                            for n in range(2):
                                last = nc.tensor.matmul(acc[2 * b + n][:, :], diag[:, k, :],
                                                        ring[:, STEPS + k, n * CH:(n + 1) * CH],
                                                        start=False, stop=True, skip_group_check=True)
                            if k % HALF == HALF - 1:
                                last.then_inc(v_used, 1)
                elif kind == "ZPROJ":
                    tall(bank, chunk, hT, args[0])
                elif kind == "MIXG":
                    pe.wait_ge(v_ready, args[0] + 1)
                    own_copies(bank - 1, 1)
                    for k in range(4):
                        w = claim_bank(pe, bank + k)
                        for g in (2 * k, 2 * k + 1):
                            last = nc.tensor.matmul(w[:, g % 2 * SGC:(g % 2 + 1) * SGC], spatialT[:, g, :],
                                                    z[:, SGW + g * SGC:SGW + (g + 1) * SGC], start=True, stop=True)
                        last.then_inc(full[(bank + k) % WB], 1)
                elif kind == "MIXT":
                    own_copies(bank - 4, 4)
                    for k in range(4):
                        w = claim_bank(pe, bank + k)
                        for c in range(4):
                            last = transpose(w[:, c * P:(c + 1) * P], z[:, (4 * k + c) * P:(4 * k + c + 1) * P])
                        last.then_inc(full[(bank + k) % WB], 1)
                    own_copies(bank, 4)
                elif kind == "MIXO":
                    b, n = args
                    for kh in range(2):
                        wt = await_chunk(pe, chunk + kh)
                        w = claim_bank(pe, bank) if kh == 0 else w
                        for k in range(KT):
                            last = nc.tensor.matmul(w[:, :], mixT1[:, kh * KT + k, :], wt[:, k, :],
                                                    start=(kh + k == 0), stop=(kh == 1 and k == KT - 1))
                        last.then_inc(full[bank % WB] if kh else half_used, 1)


_INS = ["x", "norm_mix", "norm_ffn", "ab_w_in", "ab_w_alpha2", "ab_b_alpha2", "ab_gla_norm", "ab_w_out",
        "c_w_in", "c_v_norm", "c_w_spatial", "c_b_spatial", "c_w_out", "peer_w_q", "peer_subkeys",
        "peer_u", "peer_v", "final_norm"]


def kernel(**inputs):
    import numpy as _np
    import concourse.bacc as _bacc
    from concourse import mybir as _mybir
    from concourse.bass_utils import run_bass_kernel_spmd as _run

    nc = _bacc.Bacc("TRN2", target_bir_lowering=False, num_devices=1)
    arrays, args = {}, []
    for name in _INS:
        a = _np.ascontiguousarray(inputs[name])
        arrays[f"in_{name}"] = a
        args.append(nc.dram_tensor(f"in_{name}", a.shape, _mybir.dt.from_np(a.dtype), kind="ExternalInput").ap())
    out = nc.dram_tensor("out", (1, T, D), _mybir.dt.float32, kind="ExternalOutput").ap()
    trunk(nc, *args, out)
    r = _run(nc, [arrays], core_ids=[0])
    return r.results[0]["out"]
```

```python
import concourse.bass as bass
from concourse import mybir
from collections import namedtuple
from contextlib import ExitStack

P = 128
NBLK = 2
T = P * NBLK
D = 1024
KT = D // P
CH = 512
EPS = 1e-6
SBH, SBD = 8, 64
GH, GDK, GDV, GC = 4, 64, 128, 64
RANK = 16
GATE_NORM = 16.0
SGW, SGG, SGC = 2048, 8, 256
PH, TOPK, NK = 8, 16, 128
NE = PH * TOPK
NEG = -1.0e30
LOWEST = -3.0e38

STEPS = 8
HALF = STEPS // 2
TURNS = NE // STEPS
PARTS = 4
PART_TURNS = TURNS // PARTS
HEAD_TURNS = TURNS // PH
PHEADS = PH // PARTS
PQ = 2 * PHEADS
WB = 4


B_Z, B_E, B_G = [None], [], []
_n = 0
for _hd in range(SBH):
    if _hd + 1 < SBH:
        B_Z.append(_n)
        _n += 1
    B_E.append(_n)
    B_G.append(_n + 1)
    _n += 2
    if _hd == SBH - 3:
        B_KD = _n
        _n += 2
    elif _hd == SBH - 2:
        B_GS = _n
        _n += NBLK
B_RANK, B_ALPHA, B_GQ, B_GK, B_GG, B_GG1, B_GV, B_GV1 = B_G
B_KV = _n
B_SO = B_KV + 3
MIX0_BANKS = B_SO + 2
N_CONSTS = 4
N_MASKS = 16
IDENT_MASKS = 2
N_GAINS = 2 * KT + GH
LAST_COL = 11
VNORM_COL = 14


def banks_of(kind, args):
    return {"SPATIAL": lambda: 2, "TRANSPOSE": lambda: 2 * len(args[0]), "MIX0": lambda: MIX0_BANKS,
            "PROJQK": lambda: 4, "PROJV": lambda: NBLK, "GLAREAD": lambda: NBLK, "GLAOUT": lambda: 1, "GAINS": lambda: 1, "STICK0": lambda: 1,
            "QKEYS": lambda: 4, "QPROD": lambda: len(args[1]), "QDOT": lambda: len(args[1]),
            "ZPROJ": lambda: 1, "MIXG": lambda: 1, "MIXT": lambda: 1, "MIXO": lambda: 1,
            }.get(kind, lambda: 0)()


TAKES = {"HTAKE": "TRANSPOSE", "STAKE": "SPATIAL", "KTAKE": "QKEYS", "QTAKE": "QPROD", "DTAKE": "QDOT",
         "ZTAKE": "ZPROJ", "GTAKE": "MIXG", "TTAKE": "MIXT", "OTAKE": "MIXO"}


def in_place_of_its_own(kind, args):
    return kind == "QPROD" and args[0] == 0 and args[2] == 0


def chunks_of(kind, args):
    if in_place_of_its_own(kind, args):
        return 0
    return {"PROJQK": 2, "PROJV": 1, "MIX0": 5, "QPROD": 1, "ZPROJ": 1, "MIXO": 2}.get(kind, 0)


ALL = tuple(range(PHEADS))


def gather_with(layer, b, *others):
    out, at = [("ACC", layer, b)], 0
    for turn in range(TURNS):
        behind = [stage for o in others for stage in o.get(turn, ())]
        if behind or (turn + 1) % PART_TURNS == 0:
            out.append(("GATHER", layer, b, at, turn + 1))
            out += behind
            at = turn + 1
    return out + [("FINISH",) if (layer, b) == (1, NBLK - 1) else ("ADD", layer, b)]


def transposed(norm, *blocks):
    return [("TRANSPOSE", blocks, norm), ("HTAKE", blocks, norm)]


def scored(layer, blocks, m, heads):
    q = (layer, blocks, m, heads)
    return [("QPROD", *q), ("QTAKE", *q), ("QDOT", *q)]


def trunk_for(b):
    z = [4, 5, 6, 7, 0, 1, 2, 3]
    after = {t: [] for t in range(TURNS)}
    if b == 0:
        after[0] += [("QKEYS", 1)]
        after[1] += [("KTAKE", 1)]
    after[0] += [("NORM", "mix1", (b,))]
    after[1] += transposed("mix1", b)
    for i, j in enumerate(z):
        after[2 + i] += [("ZTAKE", b, j)]
        after[1 + i] += [("ZPROJ", b, j)]
    after[5] += [("VNORM", b)]
    for k in range(4):
        after[6 + k] += [("MIXG", b, k)]
        after[7 + k] += [("GTAKE", b, k)]
    after[9] += [("MIXT", b, 0), ("MIXT", b, 1)]
    after[10] += [("TTAKE", b, 0), ("TTAKE", b, 1), ("MIXT", b, 2), ("MIXT", b, 3),
                  ("TTAKE", b, 2), ("TTAKE", b, 3), ("MIXO", b, 0)]
    after[11] += [("OTAKE", b, 0), ("MIXO", b, 1)]
    after[12] += [("OTAKE", b, 1), ("NORM", "ffn1", (b,)), ("TRANSPOSE", (b,), "ffn1")]
    after[13] += [("HTAKE", (b,), "ffn1")] + scored(1, (b,), 0, ALL)
    after[14] += [("DTAKE", 1, (b,), 0, ALL), ("TOPK", 1, b, 0), ("QPROD", 1, (b,), 1, ALL)]
    after[15] += [("TOPK", 1, b, 1), ("QTAKE", 1, (b,), 1, ALL), ("QDOT", 1, (b,), 1, ALL)]
    return after


def parts_for(b):
    q = [(1, (b,), m, ALL) for m in range(PARTS)]
    return {0: [("DTAKE", *q[1]), ("TOPK", 1, b, 2), ("QPROD", *q[2])],
            1: [("TOPK", 1, b, 3), ("QTAKE", *q[2]), ("QDOT", *q[2])],
            2: [("DTAKE", *q[2]), ("TOPK", 1, b, 4), ("QPROD", *q[3])],
            3: [("TOPK", 1, b, 5), ("QTAKE", *q[3]), ("QDOT", *q[3])],
            4: [("DTAKE", *q[3]), ("TOPK", 1, b, 6)],
            5: [("TOPK", 1, b, 7)]}


def parts_of_layer0():
    q = [(0, (0, 1), m, ALL) for m in range(PARTS)]
    only = (0, (1,), 0, ALL)
    return {0: [("QTAKE", *q[1]), ("QDOT", *q[1])],
            1: [("DTAKE", *q[1]), ("TOPK", 0, 0, 2)],
            2: [("TOPK", 0, 0, 3)],
            3: [("TOPK", 0, 1, 2), ("QPROD", *q[2])],
            4: [("TOPK", 0, 1, 3), ("QTAKE", *q[2]), ("QDOT", *q[2])],
            5: [("DTAKE", *q[2]), ("TOPK", 0, 0, 4)],
            6: [("TOPK", 0, 0, 5), ("QPROD", *q[3])],
            7: [("TOPK", 0, 1, 4), ("QTAKE", *q[3]), ("QDOT", *q[3])],
            8: [("DTAKE", *q[3]), ("TOPK", 0, 0, 6)],
            9: [("TOPK", 0, 0, 7), ("QPROD", *only)],
            10: [("TOPK", 0, 1, 5), ("QTAKE", *only), ("QDOT", *only)],
            11: [("DTAKE", *only), ("TOPK", 0, 1, 0)],
            12: [("TOPK", 0, 1, 1)], 13: [("TOPK", 0, 1, 6)], 14: [("TOPK", 0, 1, 7)]}


PLAN = ([("GAINS",), ("NORM", "mix0", (0, 1))] + transposed("mix0", 0, 1)
        + [("PROJQK",), ("SPATIAL",), ("STAKE",), ("STICK0",), ("PROJV",), ("QKEYS", 0), ("KTAKE", 0), ("MIX0",),
           ("OUT", 0, 0, 0), ("GLAREAD",), ("OUT", 0, 1, 0), ("GLAOUT", 0), ("OUT", 0, 0, 1), ("GLAOUT", 1), ("OUT", 0, 1, 1),
           ("OADD", 0), ("NORM", "ffn0", (0,)),
           ("OUT", 1, 0, 0), ("TRANSPOSE", (0,), "ffn0"), ("HTAKE", (0,), "ffn0")]
        + scored(0, (0,), 0, (0,)) + [("DTAKE", 0, (0,), 0, (0,)), ("OUT", 1, 0, 1)]
        + scored(0, (0,), 0, (1,))
        + [("OUT", 1, 1, 0), ("OUT", 1, 1, 1), ("TOPK", 0, 0, 0), ("DTAKE", 0, (0,), 0, (1,)), ("OADD", 1), ("NORM", "ffn0", (1,))]
        + transposed("ffn0", 1) + [("TOPK", 0, 0, 1), ("QPROD", 0, (0, 1), 1, ALL)]
        + gather_with(0, 0, parts_of_layer0())
        + gather_with(0, 1, trunk_for(0))
        + gather_with(1, 0, parts_for(0), trunk_for(1))
        + gather_with(1, 1, parts_for(1), {1: [("NORM", "final", (0,)), ("STORE", 0)]}))


GAIN_SLOT = {"ffn0": (0, 1), "ffn1": (1, 1), "final": (0, 2)}

TOPK_ORDER = {stage[1:]: k for k, stage in enumerate(s for s in PLAN if s[0] == "TOPK")}

Place = namedtuple("Place", "bank chunk x_writes nat banks")


def walk():
    bank = chunk = x_writes = nat = 0
    banks = {}
    for kind, *args in PLAN:
        banks[kind, *args] = banks[TAKES[kind], *args] if kind in TAKES else bank
        yield kind, args, Place(banks[kind, *args], chunk, x_writes, nat, banks)
        bank += banks_of(kind, args)
        chunk += chunks_of(kind, args)
        x_writes += kind in ("ADD", "OADD") or (kind == "OTAKE" and args[1] == 1)
        nat += kind in ("SPATIAL", "QKEYS") or (kind, *args) == ("VNORM", 0)


def trunk(nc, x_in, norm_mix, norm_ffn, ab_w_in, ab_w_alpha2, ab_b_alpha2, ab_gla_norm, ab_w_out,
          c_w_in, c_v_norm, c_w_spatial, c_b_spatial, c_w_out,
          peer_w_q, peer_subkeys, peer_u, peer_v, final_norm, out):
    f32, i32, u32 = mybir.dt.float32, mybir.dt.int32, mybir.dt.uint32
    ALU = mybir.AluOpType
    ACT = mybir.ActivationFunctionType
    AX = mybir.AxisListType
    ctx = ExitStack()
    with ctx:
        def sb(name, shape, dt=f32):
            return ctx.enter_context(nc.sbuf_tensor(name, shape, dt))

        def sem(name):
            return ctx.enter_context(nc.semaphore(name))

        x = sb("x", [P, NBLK, D])
        h = sb("h", [P, NBLK, D])
        hT = sb("hT", [P, KT, T])
        mixT = sb("mixT", [P, KT, T])
        weights = sb("weights", [P, 2, KT, CH])
        ring = sb("ring", [P, 2 * STEPS, D])
        z = sb("z", [P, 2 * SGW])
        scores = sb("scores", [P, 2 * PH * NK])
        gain = sb("gain", [P, 2, D])
        gain_rows = sb("gain_rows", [N_GAINS, P])
        gain_cols = sb("gain_cols", [P, N_GAINS])
        nat = sb("nat", [P, 2 * PH * NK])
        keysT = sb("keysT", [P, 2 * PH, NK])
        spatialT = sb("spatialT", [P, SGG, P])
        queries = sb("queries", [P, 3, CH])
        diag = sb("diag", [P, STEPS, P])
        ident = sb("ident", [P, P])
        digits = sb("digits", [P, TOPK])
        b_spatial = sb("b_spatial", [P, SGG])
        b_alpha = sb("b_alpha", [P, 2])
        w_alpha = sb("w_alpha", [RANK, GH * GDK])
        w_rank = sb("w_rank", [P, KT, RANK])
        squares = sb("squares", [P, 16])
        roots = sb("roots", [P, 2, 16])
        scale = sb("scale", [P, 16])
        gla_stat = sb("gla_stat", [P, NBLK, 3, GH])
        alphaT = sb("alphaT", [RANK, T])
        top = sb("top", [P, 2, TOPK])
        topi = sb("topi", [P, 2, TOPK], u32)
        topf = sb("topf", [P, 2, TOPK])
        best = sb("best", [P, TOPK])
        where = sb("where", [P, TOPK], u32)
        digit = sb("digit", [P, 2, TOPK], u32)
        digitf = sb("digitf", [P, 2, TOPK])
        picked = sb("picked", [P, 2, TOPK])
        gsum = sb("gsum", [P, 2])
        experts = sb("experts", [P, NBLK, NE], i32)
        gates = sb("gates", [P, NBLK, NE])
        idx = sb("idx", [P, 2, STEPS], i32)
        dots = sb("dots", [P, STEPS])
        gelus = sb("gelus", [P, STEPS])
        wts = sb("wts", [P, STEPS])

        acc = [ctx.enter_context(nc.psum_tensor(f"acc{k}", [P, CH], f32)) for k in range(4)]
        work = [ctx.enter_context(nc.psum_tensor(f"work{k}", [P, CH], f32)) for k in range(WB)]

        def slots(k, n=1):
            return ring[:, k:k + n, :].rearrange("p a b -> p (a b)")

        first_chunk = z[:, :].rearrange("p (k n) -> p k n", n=CH)

        suffix = slots(9)[:, 768:768 + 2 * P].rearrange("p (a b) -> p a b", a=2)
        before = slots(8)[:, 512:512 + 3 * P].rearrange("p (a b) -> p a b", a=3)
        beyond = queries[:, 0, 0:3 * P].rearrange("p (a b) -> p a b", a=3)
        resets = slots(10)[:, 768:768 + T]
        qT = slots(0).rearrange("p (j t) -> p j t", t=T)
        kz = slots(1, 2).rearrange("p (j t) -> p j t", t=T)
        v_sb = slots(3).rearrange("p (b n) -> p b n", b=NBLK)
        AT = slots(4, 3).rearrange("p (j t) -> p j t", t=3 * P)
        qz = slots(7).rearrange("p (j t) -> p j t", t=T)
        kin = slots(8)[:, 0:2 * T].rearrange("p (j t) -> p j t", t=T)
        kdz = slots(9)[:, 0:768].rearrange("p (c j t) -> p c j t", c=3, j=2)
        kd = slots(10)[:, 0:768].rearrange("p (c j t) -> p c j t", c=3, j=2)
        state = slots(11)[:, 0:768].rearrange("p (c j t) -> p c j t", c=3, j=2)
        v_g = slots(12).rearrange("p (b n) -> p b n", b=NBLK)
        gg = slots(13).rearrange("p (b n) -> p b n", b=NBLK)
        og = slots(14).rearrange("p (b n) -> p b n", b=NBLK)
        scT = slots(15).rearrange("p (b j t) -> p b j t", b=NBLK, j=GH)
        za, t1, la, bc = (scores[:, k * CH:(k + 1) * CH] for k in range(4))
        eb, enb, edec = (z[:, k * CH:(k + 1) * CH] for k in range(3))
        stick = z[:, 1536:1536 + 6 * 384].rearrange("p (k s t) -> p k s t", k=3, s=2)
        mixT1 = mixT[:, :, :].rearrange("p a b -> p (a b)").rearrange("p (k t) -> p k t", t=P)

        full = [sem(f"bank_full{k}") for k in range(WB)]
        free = [sem(f"bank_free{k}") for k in range(WB)]
        chunk_in = [sem(f"chunk_in{k}") for k in range(2)]
        half_used = sem("half_used")
        first_chunk_in = sem("first_chunk_in")
        out_full = sem("out_full")
        x_in_sem = [sem(f"x_in{b}") for b in range(NBLK)]
        consts_in = sem("consts_in")
        gain_rows_in = sem("gain_rows_in")
        gain_in = [sem(f"gain_in{k}") for k in range(2)]
        nat_in = sem("nat_in")
        masks = sem("masks")
        nat_masked = sem("nat_masked")
        x_ready = sem("x_ready")
        sq_ready = sem("sq_ready")
        mean_ready = sem("mean_ready")
        root_ready = sem("root_ready")
        h_ready = sem("h_ready")
        act_link = sem("act_link")
        dve_link = sem("dve_link")
        act_out = sem("act_out")
        dve_out = sem("dve_out")
        experts_ready = sem("experts_ready")
        gates_ready = sem("gates_ready")
        gla_in = sem("gla_in")
        scores_masked = sem("scores_masked")
        gla_states = sem("gla_states")
        soft_ready = sem("soft_ready")
        log_ready = sem("log_ready")
        exp_ready = sem("exp_ready")
        prob_ready = sem("prob_ready")
        v_ready = sem("v_ready")
        u_in = [sem(f"u_in{k}") for k in range(STEPS)]
        v_in = [sem(f"v_in{k}") for k in range(STEPS)]
        dots_done = sem("dots_done")
        v_used = sem("v_used")
        gelu_done = sem("gelu_done")
        wts_ready = sem("wts_ready")
        diag_ready = sem("diag_ready")
        idx_copied = sem("idx_copied")
        pool_turn = sem("pool_turn")
        stored = sem("stored")

        def await_bank(eng, n):
            eng.wait_ge(full[n % WB], n // WB + 1)
            return work[n % WB]

        def claim_bank(eng, n):
            if n >= WB:
                eng.wait_ge(free[n % WB], n // WB)
            return work[n % WB]

        def await_chunk(eng, n):
            eng.wait_ge(chunk_in[n % 2], 16 * (n // 2 + 1))
            return weights[:, n % 2]

        def gather_turn(layer, b):
            return (2 * layer + b) * TURNS

        def score_rows(layer, b):
            return mixT[:, :, :].rearrange("p a b -> p (a b)") if (layer, b) == (0, 1) else scores[:, :]

        def head_of(tile, b, hd):
            return tile[:, b, hd * TOPK:(hd + 1) * TOPK]

        def halves(bank, n=2):
            return bank[:, :].rearrange("p (j t) -> p j t", j=n)

        u_rows = peer_u.rearrange("l e d -> (l e) d")
        v_rows = peer_v.rearrange("l e d -> (l e) d")

        block = ctx.enter_context(nc.Block())

        @block.sync
        def _(sp):
            def tiled(w, r0, c0, cols=CH):
                return w[r0:r0 + D, c0:c0 + cols].rearrange("(k p) n -> p k n", p=P)

            norms = 0
            norms_with = {}
            chunk_free = []
            nat_free = [None]

            def filled(n):
                return full[n % WB], n // WB + 1

            def load_chunk(n, src, used):
                if n >= 2:
                    sp.wait_ge(*chunk_free[n - 2])
                sp.dma_start(weights[:, n % 2, :, :], src).then_inc(chunk_in[n % 2], 16)
                chunk_free.append(used)

            def load_nat(dst, src, used):
                if nat_free[0]:
                    sp.wait_ge(*nat_free[0])
                sp.dma_start(dst, src).then_inc(nat_in, 16)
                nat_free[0] = used

            halves_used = 0
            for kind, args, at in walk():
                bank, chunk = at.bank, at.chunk
                if kind == "GAINS":
                    for rows, src in ((slice(0, 2 * KT), norm_mix.rearrange("l (k p) -> (l k) p", p=P)),
                                      (slice(2 * KT, N_GAINS), ab_gla_norm.rearrange("l (k p) -> (l k) p", p=P))):
                        sp.dma_start(gain_rows[rows, :], src).then_inc(gain_rows_in, 16)
                elif kind == "NORM":
                    name = args[0]
                    if name in GAIN_SLOT and name not in norms_with:
                        if name == "final":
                            sp.wait_ge(h_ready, norms_with["ffn0"])
                        src = {"ffn0": norm_ffn[0], "ffn1": norm_ffn[1], "final": final_norm}[name]
                        slot = GAIN_SLOT[name][0]
                        sp.dma_start(gain[:, slot, :], src.partition_broadcast(P)).then_inc(gain_in[slot], 16)
                    norms += len(args[1])
                    norms_with[name] = norms
                elif kind == "PROJQK":
                    for j in range(2):
                        load_chunk(chunk + j, tiled(ab_w_in[0], 0, j * CH), filled(bank + 2 * j + 1))
                    sp.dma_start(w_rank[:, :, :], tiled(ab_w_in[0], 0, 6 * CH, RANK)).then_inc(consts_in, 16)
                elif kind == "PROJV":
                    load_chunk(chunk, tiled(ab_w_in[0], 0, 2 * CH), filled(bank + 1))
                elif kind == "MIX0":
                    for j, (cols, last) in enumerate(((3, B_GK), (5, B_GG1), (4, B_GV1))):
                        load_chunk(chunk + j, tiled(ab_w_in[0], 0, cols * CH), filled(bank + last))
                    for n in range(2):
                        load_chunk(chunk + 3 + n, tiled(ab_w_out[0], 0, n * CH), (out_full, 3 + n))
                elif kind == "GLAREAD":
                    sp.wait_ge(*filled(bank + 1))
                    sp.dma_start(first_chunk, tiled(peer_w_q[0], 0, 0)).then_inc(first_chunk_in, 16)
                elif kind == "SPATIAL":
                    load_nat(nat[:, 0:SGG * P].rearrange("t (g s) -> t g s", g=SGG),
                             c_w_spatial[0].rearrange("g t s -> t g s"), filled(bank + 1))
                elif kind == "QKEYS":
                    load_nat(nat[:, :].rearrange("n (g d) -> n g d", d=NK),
                             peer_subkeys[args[0]].rearrange("h q n d -> n (h q) d"), filled(bank + 3))
                elif kind == "QPROD" and not in_place_of_its_own(kind, args):
                    load_chunk(chunk, tiled(peer_w_q[args[0]], 0, args[2] * CH), filled(bank + len(args[1]) - 1))
                elif (kind, *args) == ("VNORM", 0):
                    load_nat(nat[:, :], c_v_norm[0].partition_broadcast(P), None)
                elif kind == "ZPROJ":
                    load_chunk(chunk, tiled(c_w_in[0], 0, args[1] * CH), filled(bank))
                elif kind == "MIXO":
                    halves_used += 1
                    for kh in range(2):
                        load_chunk(chunk + kh, tiled(c_w_out[0], kh * D, args[1] * CH),
                                   filled(bank) if kh else (half_used, halves_used))
                elif kind == "FINISH":
                    for n in range(2):
                        sp.wait_ge(h_ready, norms + n + 1)
                        sp.dma_start(out[0, (NBLK - 1) * P:, n * CH:(n + 1) * CH], h[:, NBLK - 1, n * CH:(n + 1) * CH])\
                            .then_inc(stored, 16)
                elif kind == "STORE":
                    sp.wait_ge(h_ready, norms)
                    sp.dma_start(out[0, args[0] * P:(args[0] + 1) * P, :], h[:, args[0], :]).then_inc(stored, 16)
            sp.wait_ge(stored, 16 * (NBLK + 1))

        @block.gpsimd
        def _(pool):
            step = [0]

            def after(ins):
                step[0] += 1
                ins.then_inc(masks, 1)

            after(pool.memset(ident[:, :], 0.0))
            pool.wait_ge(masks, 1)
            after(pool.affine_select(out=ident[:, :], in_=ident[:, :], compare_op=ALU.not_equal, fill=1.0,
                                     base=0, pattern=[[-1, P]], channel_multiplier=1))
            assert step[0] == IDENT_MASKS
            for tile, value in ((suffix, -1.0), (before, 1.0), (beyond, 0.0), (resets, 1.0)):
                after(pool.memset(tile, value))
            for tile in (kz, qz, kdz):
                after(pool.memset(tile, 0.0))
            pool.wait_ge(masks, step[0])
            after(pool.affine_select(out=suffix[:, 0, :], in_=suffix[:, 0, :], compare_op=ALU.is_ge, fill=0.0,
                                     base=0, pattern=[[-1, P]], channel_multiplier=1))
            for part in (0, 2):
                after(pool.affine_select(out=before[:, part, :], in_=before[:, part, :], compare_op=ALU.is_gt,
                                         fill=0.0, base=0, pattern=[[1, P]], channel_multiplier=-1))
                after(pool.affine_select(out=beyond[:, part, :], in_=beyond[:, part, :], compare_op=ALU.is_gt,
                                         fill=NEG, base=0, pattern=[[1, P]], channel_multiplier=-1))
            after(pool.affine_select(out=resets[:, :].rearrange("p (c t) -> p c t", t=GC),
                                     in_=resets[:, :].rearrange("p (c t) -> p c t", t=GC),
                                     compare_op=ALU.not_equal, fill=0.0, base=0,
                                     pattern=[[0, T // GC], [1, GC]], channel_multiplier=0))
            after(pool.iota(digits[:, :], pattern=[[1, TOPK]], base=0, channel_multiplier=0,
                            allow_small_or_imprecise_dtypes=True))
            assert step[0] == N_MASKS

            for kind, args, at in walk():
                bank, chunk = at.bank, at.chunk
                if kind == "SPATIAL":
                    pool.wait_ge(nat_in, 16)
                    m = nat[:, 0:SGG * P].rearrange("t (g s) -> t g s", g=SGG)
                    pool.affine_select(out=m, in_=m, compare_op=ALU.is_ge, fill=0.0, base=0,
                                       pattern=[[0, SGG], [-1, P]], channel_multiplier=1).then_inc(nat_masked, 1)
                elif kind == "MIX0":
                    for b in range(NBLK):
                        n = bank + B_GS + b
                        pool.wait_ge(free[n % WB], n // WB + 1)
                        pool.affine_select(out=scT[:, b], in_=scT[:, b], compare_op=ALU.is_ge, fill=0.0, base=0,
                                           pattern=[[0, GH], [1, P]], channel_multiplier=-1).then_inc(scores_masked, 1)
                        pool.wait_ge(scores_masked, 2 * b + 1)
                        pool.memset(scT[0:GC, b, :, GC:P], 0.0).then_inc(scores_masked, 1)
                elif kind == "GATHER":
                    layer, b, i0, i1 = args
                    t0 = gather_turn(layer, b)
                    ahead = range(i0, min(i1 + 1, TURNS))
                    pool.wait_ge(experts_ready, 1 + max(TOPK_ORDER[layer, b, i // HEAD_TURNS] for i in ahead))

                    def fetch(t, i, g, copies):
                        table, used, landed = ((u_rows, dots_done, u_in), (v_rows, v_used, v_in))[t]
                        pool.wait_ge(used, 2 * (t0 + i) + g + 1)
                        pool.sem_inc(pool_turn, 1)
                        pool.tensor_copy(idx[:, t, g * HALF:(g + 1) * HALF],
                                         experts[:, b, bass.ds(i * STEPS + g * HALF, HALF)]).then_inc(idx_copied, 1)
                        pool.wait_ge(idx_copied, copies + 1)
                        pool.sem_inc(pool_turn, 1)
                        for k in range(g * HALF, (g + 1) * HALF):
                            pool.indirect_dma_start(
                                ring[:, t * STEPS + k, :], None, table,
                                bass.IndirectOffsetOnAxis(ap=idx[:, t, k:k + 1], axis=0)).then_inc(landed[k], 16)

                    if i0 == 0:
                        fetch(0, 0, 0, 4 * t0)
                    if i0 < TURNS - 1:
                        with pool.Fori(i0, min(i1, TURNS - 1)) as i:
                            fetch(0, i, 1, 4 * (t0 + i) + 1)
                            fetch(1, i, 0, 4 * (t0 + i) + 2)
                            fetch(0, i + 1, 0, 4 * (t0 + i) + 3)
                            fetch(1, i, 1, 4 * (t0 + i) + 4)
                    if i1 == TURNS:
                        i = TURNS - 1
                        fetch(0, i, 1, 4 * (t0 + i) + 1)
                        fetch(1, i, 0, 4 * (t0 + i) + 2)
                        fetch(1, i, 1, 4 * (t0 + i) + 3)

        @block.scalar
        def _(act):
            links = [0]
            seen = {"dve": 0, "norm": 0}

            def link(ins):
                links[0] += 1
                ins.then_inc(act_link, 1)
                act.wait_ge(act_link, links[0])

            def await_dve():
                seen["dve"] += 1
                act.wait_ge(dve_out, seen["dve"])

            def norm(b, x_writes):
                k = seen["norm"]
                seen["norm"] += 1
                if k < NBLK:
                    act.wait_ge(x_in_sem[b], 16)
                else:
                    act.wait_ge(x_ready, x_writes)
                nc.scalar.activation(h[:, b, :], x[:, b, :], ACT.Square,
                                     accum_out=squares[:, k:k + 1]).then_inc(sq_ready, 1)
                act.wait_ge(mean_ready, k + 1)
                nc.scalar.activation(roots[:, 1, k:k + 1], roots[:, 0, k:k + 1], ACT.Sqrt).then_inc(root_ready, 1)

            def take_hT(n, b):
                for half in range(2):
                    w = await_bank(act, n + half)
                    nc.scalar.activation(hT[:, half * 4:half * 4 + 4, b * P:(b + 1) * P], halves(w, 4), ACT.Copy)\
                        .then_inc(free[(n + half) % WB], 1)

            for b in range(NBLK):
                act.dma_start(x[:, b, :], x_in[0, b * P:(b + 1) * P, :]).then_inc(x_in_sem[b], 16)
            act.dma_start(w_alpha[:, :], ab_w_alpha2[0]).then_inc(consts_in, 16)
            act.dma_start(b_alpha[:, :], ab_b_alpha2[0].rearrange("(j p) -> p j", p=P),
                          allow_slow_non_contiguous=True).then_inc(consts_in, 16)
            act.dma_start(b_spatial[:, :], c_b_spatial[0].rearrange("g t -> t g"),
                          allow_slow_non_contiguous=True).then_inc(consts_in, 16)

            def mix0(n0):
                for hd in range(SBH):
                    if hd + 1 < SBH:
                        stick_soft(n0 + B_Z[hd + 1], hd + 1)
                    stick_prob(hd)
                    gla_piece(n0, n0 + B_G[hd])
                    if hd == SBH - 3:
                        for k in range(2):
                            w = await_bank(act, n0 + B_KD + k)
                            n = 4 if k == 0 else 2
                            dst = kd[:, 2 * k:2 * k + n // 2].rearrange("p c j t -> p (c j t)")
                            nc.scalar.activation(dst, w[:, 0:n * P], ACT.Copy).then_inc(free[(n0 + B_KD + k) % WB], 1)
                    elif hd == SBH - 2:
                        for b in range(NBLK):
                            w = await_bank(act, n0 + B_GS + b)
                            nc.scalar.activation(scT[:, b], halves(w, GH), ACT.Copy).then_inc(free[(n0 + B_GS + b) % WB], 1)
                for k in range(2):
                    n = n0 + B_SO + k
                    w = await_bank(act, n)
                    nc.scalar.activation(mixT[:, 2 * k:2 * k + 2, :], halves(w), ACT.Copy).then_inc(free[n % WB], 1)

            def gla_piece(n0, n):
                if n == n0 + B_RANK:
                    w = await_bank(act, n)
                    nc.scalar.activation(alphaT[:, :], w[0:RANK, 0:T], ACT.Copy).then_inc(free[n % WB], 1)
                elif n == n0 + B_ALPHA:
                    w = await_bank(act, n)
                    act.wait_ge(consts_in, 16 * N_CONSTS)
                    for j in range(2):
                        last = nc.scalar.activation(za[:, j * T:(j + 1) * T], w[:, j * T:(j + 1) * T], ACT.Identity,
                                                    bias=b_alpha[:, j:j + 1])
                    link(last)
                    act.sem_inc(free[n % WB], 1)
                    link(nc.scalar.activation(t1, za, ACT.Abs))
                    link(nc.scalar.activation(t1, t1, ACT.Exp, scale=-1.0))
                    nc.scalar.activation(t1, t1, ACT.Ln, bias=1.0).then_inc(act_out, 1)
                elif n == n0 + B_GQ:
                    await_dve()
                    nc.scalar.activation(eb, bc, ACT.Exp, scale=1.0 / GATE_NORM)
                    nc.scalar.activation(enb, bc, ACT.Exp, scale=-1.0 / GATE_NORM)
                    nc.scalar.activation(edec, t1, ACT.Exp, scale=1.0 / GATE_NORM).then_inc(act_out, 1)
                elif n in (n0 + B_GV, n0 + B_GV1):
                    w = await_bank(act, n)
                    nc.scalar.activation(v_g[:, int(n != n0 + B_GV), :], w[:, :], ACT.Copy).then_inc(free[n % WB], 1)
                elif n in (n0 + B_GG, n0 + B_GG1):
                    w = await_bank(act, n)
                    nc.scalar.activation(gg[:, int(n == n0 + B_GG1), :], w[:, :], ACT.Sigmoid).then_inc(act_out, 1)

            def stick_soft(n, hd):
                w = await_bank(act, n)
                s = stick[:, 0, hd % 2, :]
                if hd >= 2:
                    act.wait_ge(log_ready, hd - 1)
                link(nc.scalar.activation(s, w[:, 0:3 * P], ACT.Abs))
                link(nc.scalar.activation(s, s, ACT.Exp, scale=-1.0))
                nc.scalar.activation(s, s, ACT.Ln, bias=1.0).then_inc(soft_ready, 1)

            def stick_prob(hd):
                act.wait_ge(exp_ready, hd + 1)
                nc.scalar.activation(AT[:, hd, :], stick[:, 2, hd % 2, :], ACT.Exp).then_inc(prob_ready, 1)

            for kind, args, at in walk():
                bank, chunk = at.bank, at.chunk
                if kind == "PROJQK":
                    for j in range(2):
                        w = await_bank(act, bank + j)
                        nc.scalar.activation(qT[:, 2 * j:2 * j + 2, :], halves(w), ACT.Copy, scale=SBD ** -0.5)\
                            .then_inc(free[(bank + j) % WB], 1)
                    act.wait_ge(masks, N_MASKS)
                    w = halves(await_bank(act, bank + 3))
                    for j in range(2):
                        for r in range(2):
                            rows = slice(64 * r, 64 * r + 64)
                            last = nc.scalar.activation(kz[rows, 4 + 2 * j + r, :], w[rows, j, :], ACT.Copy)
                    last.then_inc(free[(bank + 3) % WB], 1)
                elif kind == "STICK0":
                    stick_soft(bank, 0)
                elif kind == "PROJV":
                    for b in range(NBLK):
                        w = await_bank(act, bank + b)
                        nc.scalar.activation(v_sb[:, b, :], w[:, :], ACT.Copy).then_inc(free[(bank + b) % WB], 1)
                elif kind == "MIX0":
                    mix0(bank)
                elif kind == "GLAOUT":
                    b = args[0]
                    w = await_bank(act, at.banks["GLAREAD",] + b)
                    for hd in range(GH):
                        last = nc.scalar.activation(og[:, b, hd * GDV:(hd + 1) * GDV], w[:, hd * GDV:(hd + 1) * GDV],
                                                    ACT.Square, accum_out=gla_stat[:, b, 0, hd:hd + 1])
                    last.then_inc(act_out, 1)
                    await_dve()
                    nc.scalar.activation(gla_stat[:, b, 2, :], gla_stat[:, b, 1, :], ACT.Sqrt).then_inc(act_out, 1)
                elif kind == "NORM":
                    for b in args[1]:
                        norm(b, at.x_writes)
                elif kind == "HTAKE" and not args[1].startswith("mix"):
                    for k, b in enumerate(args[0]):
                        take_hT(bank + 2 * k, b)
                elif kind == "QTAKE":
                    width = len(args[3]) * 2 * P
                    for n in range(bank, bank + len(args[1])):
                        w = await_bank(act, n)
                        nc.scalar.activation(queries[:, n % 3, 0:width], w[:, 0:width], ACT.Copy).then_inc(free[n % WB], 1)
                elif kind == "DTAKE":
                    layer, blocks, m, heads = args
                    width, at0 = len(heads) * 2 * NK, (m * PHEADS + heads[0]) * 2 * NK
                    for k, b in enumerate(blocks):
                        n = bank + k
                        w = await_bank(act, n)
                        nc.scalar.activation(score_rows(layer, b)[:, at0:at0 + width], w[:, 0:width], ACT.Copy).then_inc(free[n % WB], 1)
                elif kind == "TOPK":
                    await_dve()
                    g = head_of(gates, args[1], args[2])
                    nc.scalar.activation(g, g, ACT.Exp).then_inc(act_out, 1)
                elif kind == "GATHER":
                    layer, b, i0, i1 = args
                    t0 = gather_turn(layer, b)
                    with act.Fori(i0, i1) as i:
                        for g in range(2):
                            now = 2 * (t0 + i) + g + 1
                            part = slice(g * HALF, (g + 1) * HALF)
                            act.wait_ge(dots_done, now + 2)
                            nc.scalar.activation(gelus[:, part], dots[:, part], ACT.Gelu).then_inc(gelu_done, 1)
                            act.wait_ge(wts_ready, now)
                            act.wait_ge(v_used, now)
                            for k in range(g * HALF, (g + 1) * HALF):
                                last = nc.scalar.activation(diag[:, k, :], ident[:, :], ACT.Copy, scale=wts[:, k:k + 1])
                            last.then_inc(diag_ready, 1)
                elif kind == "FINISH":
                    b = NBLK - 1
                    act.wait_ge(v_used, 2 * gather_turn(2, 0) + 2)
                    for n in range(2):
                        last = nc.scalar.activation(h[:, b, n * CH:(n + 1) * CH], acc[2 * b + n][:, :], ACT.Square,
                                                    accum_out=squares[:, LAST_COL + n:LAST_COL + n + 1])
                    last.then_inc(act_out, 1)
                    await_dve()
                    k = LAST_COL
                    nc.scalar.activation(roots[:, 1, k:k + 1], roots[:, 0, k:k + 1], ACT.Sqrt).then_inc(act_out, 1)
                elif kind == "ZTAKE":
                    w = await_bank(act, bank)
                    cols = slice(args[1] * CH, (args[1] + 1) * CH)
                    nc.scalar.activation(z[:, cols], w[:, :], ACT.Gelu).then_inc(free[bank % WB], 1)
                elif kind == "VNORM":
                    for j in range(4, 8):
                        n = at.banks["ZPROJ", args[0], j]
                        act.wait_ge(free[n % WB], n // WB + 1)
                    k = VNORM_COL + args[0]
                    nc.scalar.activation(mixT[:, :, :].rearrange("p a b -> p (a b)"), z[:, SGW:2 * SGW], ACT.Square,
                                         accum_out=squares[:, k:k + 1]).then_inc(act_out, 1)
                    await_dve()
                    nc.scalar.activation(roots[:, 1, k:k + 1], roots[:, 0, k:k + 1], ACT.Sqrt).then_inc(act_out, 1)
                elif kind == "TTAKE":
                    w = await_bank(act, bank)
                    nc.scalar.activation(mixT1[:, 4 * args[1]:4 * args[1] + 4, :], halves(w, 4), ACT.Copy)\
                        .then_inc(free[bank % WB], 1)

        @block.vector
        def _(dve):
            links = [0]
            seen = {"act": 0, "norm": 0}
            scores_bank = {}

            def link(ins):
                links[0] += 1
                ins.then_inc(dve_link, 1)
                dve.wait_ge(dve_link, links[0])

            def await_act():
                seen["act"] += 1
                dve.wait_ge(act_out, seen["act"])

            def norm(b, name):
                k = seen["norm"]
                seen["norm"] += 1
                dve.wait_ge(sq_ready, k + 1)
                nc.vector.tensor_scalar(roots[:, 0, k:k + 1], squares[:, k:k + 1], 1.0 / D, EPS, ALU.mult, ALU.add)\
                    .then_inc(mean_ready, 1)
                dve.wait_ge(root_ready, k + 1)
                link(nc.vector.reciprocal(scale[:, k:k + 1], roots[:, 1, k:k + 1]))
                if name not in GAIN_SLOT:
                    nc.vector.tensor_scalar(h[:, b, :], x[:, b, :], scale[:, k:k + 1], None, ALU.mult).then_inc(h_ready, 1)
                    return
                slot, loads = GAIN_SLOT[name]
                dve.wait_ge(gain_in[slot], 16 * loads)
                nc.vector.scalar_tensor_tensor(h[:, b, :], x[:, b, :], scale[:, k:k + 1], gain[:, slot, :],
                                               ALU.mult, ALU.mult).then_inc(h_ready, 1)

            def take_transposed(dst, n, count):
                for k in range(count):
                    w = await_bank(dve, n + k)
                    nc.vector.tensor_copy(dst[:, 4 * k:4 * k + 4, :], halves(w, 4)).then_inc(free[(n + k) % WB], 1)

            def take_keys(n0):
                dve.wait_ge(masks, N_MASKS)
                w = halves(await_bank(dve, n0))
                for j in range(2):
                    for r in range(2):
                        rows = slice(64 * r, 64 * r + 64)
                        last = nc.vector.tensor_copy(kz[rows, 2 * j + r, :], w[rows, j, :])
                last.then_inc(free[n0 % WB], 1)

            def mix0(n0):
                for hd in range(SBH):
                    stick_mask(n0 + B_E[hd], hd)
                    if hd + 1 < SBH:
                        stick_log(n0 + B_Z[hd + 1], hd + 1)
                    gla_piece(n0, n0 + B_G[hd])
                gla_carry(n0 + B_KV)

            q_raw, k_raw = scT[:, 0].rearrange("p j t -> p (j t)"), scT[:, 1].rearrange("p j t -> p (j t)")

            def gla_piece(n0, n):
                if n == n0 + B_ALPHA:
                    await_act()
                    link(nc.vector.scalar_tensor_tensor(la, za, 0.0, t1, ALU.min, ALU.subtract))
                    for j in range(2):
                        last = nc.vector.tensor_tensor_scan(bc[:, j * T:(j + 1) * T], resets[:, :], la[:, j * T:(j + 1) * T],
                                                            0.0, ALU.mult, ALU.add)
                    link(last)
                    shape = [P, 2 * T // GC, GC]
                    bcc = bc.rearrange("p (c t) -> p c t", t=GC)
                    nc.vector.tensor_tensor(t1.rearrange("p (c t) -> p c t", t=GC), bcc[:, :, GC - 1:GC].to_broadcast(shape),
                                            bcc, ALU.subtract).then_inc(dve_out, 1)
                elif n == n0 + B_GQ:
                    w = await_bank(dve, n)
                    link(nc.vector.tensor_copy(q_raw, w[:, :]))
                    dve.sem_inc(free[n % WB], 1)
                elif n == n0 + B_GK:
                    w = await_bank(dve, n)
                    link(nc.vector.tensor_copy(k_raw, w[:, :]))
                    dve.sem_inc(free[n % WB], 1)
                    gla_gated()
                elif n in (n0 + B_GG, n0 + B_GG1):
                    await_act()
                    g, w = gg[:, int(n == n0 + B_GG1), :], work[n % WB]
                    link(nc.vector.tensor_tensor(g, g, w[:, :], ALU.mult))
                    dve.sem_inc(free[n % WB], 1)

            def gla_gated():
                await_act()
                for hd in range(GH):
                    j, rows = hd // 2, slice(64 * (hd % 2), 64 * (hd % 2) + 64)
                    nc.vector.scalar_tensor_tensor(qz[rows, hd, :], q_raw[rows, j * T:(j + 1) * T], GDK ** -0.5,
                                                   eb[rows, j * T:(j + 1) * T], ALU.mult, ALU.mult)
                nc.vector.tensor_tensor(kin.rearrange("p j t -> p (j t)"), k_raw, enb, ALU.mult)
                for c in range(3):
                    cols = slice(c * GC, (c + 1) * GC)
                    at = c % 2 * GC
                    last = nc.vector.tensor_tensor(kdz[:, c, :, at:at + GC],
                                                   k_raw.rearrange("p (j t) -> p j t", t=T)[:, :, cols],
                                                   edec.rearrange("p (j t) -> p j t", t=T)[:, :, cols], ALU.mult)
                last.then_inc(gla_in, 1)

            def gla_carry(n0):
                for c in range(3):
                    n = n0 + c
                    w = await_bank(dve, n)
                    for j in range(2):
                        for r in range(2):
                            rows = slice(64 * r, 64 * r + 64)
                            new = w[rows, j * T + r * GDV:j * T + (r + 1) * GDV]
                            if c == 0:
                                last = nc.vector.tensor_copy(state[rows, c, j, :], new)
                            else:
                                e = j * T + c * GC + GC - 1
                                last = nc.vector.scalar_tensor_tensor(state[rows, c, j, :], state[rows, c - 1, j, :],
                                                                      eb[rows, e:e + 1], new, ALU.mult, ALU.add)
                    last.then_inc(gla_states, 1)
                    dve.wait_ge(gla_states, c + 1)
                    dve.sem_inc(free[n % WB], 1)

            def gla_norm(n, b):
                await_act()
                nc.vector.tensor_scalar(gla_stat[:, b, 1, :], gla_stat[:, b, 0, :], 1.0 / GDV, EPS, ALU.mult, ALU.add)\
                    .then_inc(dve_out, 1)
                await_act()
                link(nc.vector.reciprocal(gla_stat[:, b, 1, :], gla_stat[:, b, 2, :]))
                w = work[n % WB]
                for hd in range(GH):
                    cols = slice(hd * GDV, (hd + 1) * GDV)
                    last = nc.vector.scalar_tensor_tensor(og[:, b, cols], w[:, cols], gla_stat[:, b, 1, hd:hd + 1],
                                                          gg[:, b, cols], ALU.mult, ALU.mult)
                last.then_inc(free[n % WB], 1)

            def stick_log(n, hd):
                dve.wait_ge(soft_ready, hd + 1)
                s = stick[:, 1, hd % 2, :]
                link(nc.vector.scalar_tensor_tensor(s, work[n % WB][:, 0:3 * P], 0.0, stick[:, 0, hd % 2, :], ALU.max, ALU.add))
                dve.sem_inc(free[n % WB], 1)
                nc.vector.tensor_tensor(s, s, before.rearrange("p a b -> p (a b)"), ALU.mult).then_inc(log_ready, 1)

            def stick_mask(n, hd):
                w = await_bank(dve, n)
                if hd >= 2:
                    dve.wait_ge(prob_ready, hd - 1)
                nc.vector.tensor_tensor(stick[:, 2, hd % 2, :], w[:, 0:3 * P],
                                        beyond.rearrange("p a b -> p (a b)"), ALU.add).then_inc(exp_ready, 1)
                dve.wait_ge(exp_ready, hd + 1)
                dve.sem_inc(free[n % WB], 1)

            def top16(values, out_v, out_i, rows):
                for k in range(rows):
                    last = nc.vector.max(out_v[:, k, 0:8], values[:, k, :])
                link(last)
                for k in range(rows):
                    nc.vector.max_index(out_i[:, k, 0:8], out_v[:, k, 0:8], values[:, k, :])
                for k in range(rows):
                    last = nc.vector.match_replace(values[:, k, :], out_v[:, k, 0:8], values[:, k, :], LOWEST)
                link(last)
                for k in range(rows):
                    last = nc.vector.max(out_v[:, k, 8:16], values[:, k, :])
                link(last)
                for k in range(rows):
                    last = nc.vector.max_index(out_i[:, k, 8:16], out_v[:, k, 8:16], values[:, k, :])
                link(last)

            def top_keys(rows, n):
                dve.wait_ge(free[n % WB], n // WB + 1)
                top16(rows.rearrange("p (g n) -> p g n", n=NK), top, topi, 2)

            def top_pairs(rows):
                shape = [P, TOPK, TOPK]
                link(nc.vector.tensor_tensor(rows.rearrange("p (a c) -> p a c", a=TOPK),
                                             top[:, 0, :].unsqueeze(2).to_broadcast(shape),
                                             top[:, 1, :].unsqueeze(1).to_broadcast(shape), ALU.add))
                top16(rows.unsqueeze(1), best[:, :].unsqueeze(1), where[:, :].unsqueeze(1), 1)

            def expert_ids(layer, b, hd, rows):
                nc.vector.tensor_scalar(digit[:, 0, :], where[:, :], 4, None, ALU.logical_shift_right)
                nc.vector.tensor_scalar(digit[:, 1, :], where[:, :], 15, None, ALU.bitwise_and)
                link(nc.vector.tensor_copy(topf[:, :, :], topi[:, :, :]))
                link(nc.vector.tensor_copy(digitf[:, :, :], digit[:, :, :]))
                hot = rows.rearrange("p (n a) -> p n a", a=TOPK)
                shape = [P, TOPK, TOPK]
                for q in range(2):
                    link(nc.vector.tensor_tensor(hot, digitf[:, q, :].unsqueeze(2).to_broadcast(shape),
                                                 digits[:, :].unsqueeze(1).to_broadcast(shape), ALU.is_equal))
                    link(nc.vector.tensor_tensor(hot, hot, topf[:, q, :].unsqueeze(1).to_broadcast(shape), ALU.mult))
                    link(nc.vector.tensor_reduce(picked[:, q, :], hot, AX.X, ALU.add))
                link(nc.vector.tensor_scalar(picked[:, 0, :], picked[:, 0, :], float(NK), float(layer * NK * NK),
                                             ALU.mult, ALU.add))
                nc.vector.tensor_tensor(head_of(experts, b, hd), picked[:, 0, :], picked[:, 1, :], ALU.add)\
                    .then_inc(experts_ready, 1)

            def gate_shift(b, hd):
                nc.vector.tensor_tensor(head_of(gates, b, hd), best[:, :], best[:, 0:1].to_broadcast([P, TOPK]),
                                        ALU.subtract).then_inc(dve_out, 1)

            def gate_norm(b, hd):
                g = head_of(gates, b, hd)
                await_act()
                link(nc.vector.tensor_reduce(gsum[:, 0:1], g, AX.X, ALU.add))
                link(nc.vector.reciprocal(gsum[:, 1:2], gsum[:, 0:1]))
                link(nc.vector.tensor_tensor(g, g, gsum[:, 1:2].to_broadcast([P, TOPK]), ALU.mult))

            dve.sem_inc(dots_done, 2)
            for kind, args, at in walk():
                bank, chunk = at.bank, at.chunk
                if kind == "PROJQK":
                    take_keys(bank + 2)
                elif kind == "GAINS":
                    w = await_bank(dve, bank)
                    nc.vector.tensor_copy(gain_cols[:, :], w[:, 0:N_GAINS]).then_inc(free[bank % WB], 1)
                elif kind == "STICK0":
                    stick_log(bank, 0)
                elif kind == "HTAKE" and args[1].startswith("mix"):
                    own = at.banks["GAINS",]
                    dve.wait_ge(free[own % WB], own // WB + 1)
                    g0 = int(args[1] == "mix1") * KT
                    for n in range(bank, bank + 2 * len(args[0])):
                        half, b = (n - bank) % 2, args[0][(n - bank) // 2]
                        g = g0 + half * 4
                        w = await_bank(dve, n)
                        nc.vector.tensor_tensor(hT[:, half * 4:half * 4 + 4, b * P:(b + 1) * P], halves(w, 4),
                                                gain_cols[:, g:g + 4].unsqueeze(2).to_broadcast([P, 4, P]), ALU.mult)\
                            .then_inc(free[n % WB], 1)
                elif kind == "STAKE":
                    take_transposed(spatialT, bank, 2)
                elif kind == "KTAKE":
                    take_transposed(keysT, bank, 4)
                elif kind == "MIX0":
                    mix0(bank)
                elif kind == "GLAOUT":
                    b = args[0]
                    gla_norm(at.banks["GLAREAD",] + b, b)
                    w = await_bank(dve, bank)
                    nc.vector.tensor_tensor(mixT[:, 4:8, b * P:(b + 1) * P], halves(w, GH),
                                            gain_cols[:, 2 * KT:].unsqueeze(2).to_broadcast([P, GH, P]), ALU.mult)\
                        .then_inc(free[bank % WB], 1)
                elif kind == "OADD":
                    b = args[0]
                    for n in range(2):
                        dve.wait_ge(out_full, 2 * b + n + 1)
                        xs = x[:, b, n * CH:(n + 1) * CH]
                        last = nc.vector.tensor_tensor(xs, xs, acc[2 * b + n][:, :], ALU.add)
                    last.then_inc(x_ready, 1)
                elif kind == "NORM":
                    for b in args[1]:
                        norm(b, args[0])
                elif kind == "DTAKE":
                    layer, blocks, m, heads = args
                    for k, b in enumerate(blocks):
                        for hd in heads:
                            scores_bank[layer, b, m * PHEADS + hd] = bank + k
                elif kind == "TOPK":
                    layer, b, hd = args
                    rows = score_rows(layer, b)[:, 2 * hd * NK:2 * (hd + 1) * NK]
                    top_keys(rows, scores_bank[layer, b, hd])
                    top_pairs(rows)
                    gate_shift(b, hd)
                    expert_ids(layer, b, hd, rows)
                    gate_norm(b, hd)
                elif kind == "GATHER":
                    layer, b, i0, i1 = args
                    t0 = gather_turn(layer, b)
                    with dve.Fori(i0, i1) as i:
                        def weigh(g):
                            part = slice(g * HALF, (g + 1) * HALF)
                            dve.wait_ge(gelu_done, 2 * (t0 + i) + g + 1)
                            nc.vector.tensor_tensor(wts[:, part], gelus[:, part],
                                                    gates[:, b, bass.ds(i * STEPS + g * HALF, HALF)],
                                                    ALU.mult).then_inc(wts_ready, 1)

                        for k in range(STEPS):
                            dve.wait_ge(u_in[k], 16 * (t0 + i + 1))
                            last = nc.vector.tensor_tensor_reduce(
                                out=ring[:, k, :], in0=ring[:, k, :], in1=h[:, b, :], scale=1.0, scalar=0.0,
                                op0=ALU.mult, op1=ALU.add, accum_out=dots[:, k:k + 1])
                            if k % HALF == HALF - 1:
                                last.then_inc(dots_done, 1)
                            if k == HALF:
                                weigh(0)
                        weigh(1)
                elif kind == "ADD":
                    layer, b = args
                    dve.wait_ge(v_used, 2 * (gather_turn(layer, b) + TURNS) + 2)
                    nc.vector.tensor_copy(x[:, b, 0:CH], acc[2 * b][:, :])
                    nc.vector.tensor_copy(x[:, b, CH:D], acc[2 * b + 1][:, :]).then_inc(x_ready, 1)
                elif kind == "FINISH":
                    b, k = NBLK - 1, LAST_COL
                    await_act()
                    link(nc.vector.tensor_tensor(squares[:, k:k + 1], squares[:, k:k + 1], squares[:, k + 1:k + 2], ALU.add))
                    nc.vector.tensor_scalar(roots[:, 0, k:k + 1], squares[:, k:k + 1], 1.0 / D, EPS, ALU.mult, ALU.add)\
                        .then_inc(dve_out, 1)
                    await_act()
                    link(nc.vector.reciprocal(scale[:, k:k + 1], roots[:, 1, k:k + 1]))
                    slot = GAIN_SLOT["final"][0]
                    for n in range(2):
                        cols = slice(n * CH, (n + 1) * CH)
                        nc.vector.scalar_tensor_tensor(h[:, b, cols], acc[2 * b + n][:, :], scale[:, k:k + 1],
                                                       gain[:, slot, cols], ALU.mult, ALU.mult).then_inc(h_ready, 1)
                elif kind == "VNORM":
                    b = args[0]
                    k = VNORM_COL + b
                    await_act()
                    nc.vector.tensor_scalar(roots[:, 0, k:k + 1], squares[:, k:k + 1], 1.0 / SGW, EPS, ALU.mult, ALU.add)\
                        .then_inc(dve_out, 1)
                    await_act()
                    link(nc.vector.reciprocal(scale[:, k:k + 1], roots[:, 1, k:k + 1]))
                    dve.wait_ge(nat_in, 16 * (at.nat + (b == 0)))
                    nc.vector.scalar_tensor_tensor(z[:, SGW:2 * SGW], z[:, SGW:2 * SGW], scale[:, k:k + 1],
                                                   nat[:, :], ALU.mult, ALU.mult).then_inc(v_ready, 1)
                elif kind == "GTAKE":
                    b, k = args
                    dve.wait_ge(consts_in, 16 * N_CONSTS)
                    n = at.banks["ZPROJ", b, k]
                    dve.wait_ge(free[n % WB], n // WB + 1)
                    w = await_bank(dve, bank)
                    for g in (2 * k, 2 * k + 1):
                        u = z[:, g * SGC:(g + 1) * SGC]
                        last = nc.vector.scalar_tensor_tensor(u, w[:, g % 2 * SGC:(g % 2 + 1) * SGC],
                                                              b_spatial[:, g:g + 1], u, ALU.add, ALU.mult)
                    last.then_inc(free[bank % WB], 1)
                elif kind == "OTAKE":
                    b, n = args
                    w = await_bank(dve, bank)
                    xs = x[:, b, n * CH:(n + 1) * CH]
                    link(nc.vector.tensor_tensor(xs, xs, w[:, :], ALU.add))
                    dve.sem_inc(free[bank % WB], 1)
                    if n == 1:
                        dve.sem_inc(x_ready, 1)

        @block.tensor
        def _(pe):
            seen = {"norm": 0}

            def transpose(dst, src):
                return nc.tensor.matmul(dst, src, ident[:, :], is_transpose=True, start=True, stop=True)

            def make_hT(n, b):
                seen["norm"] += 1
                pe.wait_ge(h_ready, seen["norm"])
                for half in range(2):
                    w = claim_bank(pe, n + half)
                    for c in range(4):
                        k = half * 4 + c
                        last = transpose(w[:, c * P:(c + 1) * P], h[:, b, k * P:(k + 1) * P])
                    last.then_inc(full[(n + half) % WB], 1)

            def fill_transposed(n, src):
                w = claim_bank(pe, n)
                for c in range(4):
                    last = transpose(w[:, c * P:(c + 1) * P], src[:, c * P:(c + 1) * P])
                last.then_inc(full[n % WB], 1)

            def own_copies(n, count):
                for k in range(n, n + count):
                    pe.wait_ge(free[k % WB], k // WB + 1)

            def wide(n, wt, cols, tiles=range(CH // P)):
                width = cols.stop - cols.start
                per = CH // width
                for i, t in enumerate(tiles):
                    if i % per == 0:
                        w = claim_bank(pe, n + i // per)
                    dst = w[:, i % per * width:(i % per + 1) * width]
                    for k in range(KT):
                        last = nc.tensor.matmul(dst, wt[:, k, t * P:(t + 1) * P], hT[:, k, cols],
                                                start=(k == 0), stop=(k == KT - 1))
                    if i % per == per - 1 or i == len(tiles) - 1:
                        last.then_inc(full[(n + i // per) % WB], 1)

            def tall(n, chunk, src, b):
                wt = await_chunk(pe, chunk)
                w = claim_bank(pe, n)
                for k in range(KT):
                    last = nc.tensor.matmul(w[:, :], src[:, k, b * P:(b + 1) * P], wt[:, k, :],
                                            start=(k == 0), stop=(k == KT - 1))
                last.then_inc(full[n % WB], 1)

            def mix0(n0, c0, v0):
                for hd in range(SBH):
                    if hd + 1 < SBH:
                        stick_score(n0 + B_Z[hd + 1], hd + 1)
                    stick_exponent(n0 + B_E[hd], hd)
                    n = n0 + B_G[hd]
                    if hd == 0:
                        gate_input(n)
                    elif hd == 1:
                        own_copies(n0 + B_RANK, 1)
                        gate_logits(n)
                    elif hd < 4:
                        wide(n, await_chunk(pe, c0), slice(0, T), range(2 * hd - 4, 2 * hd - 2))
                    else:
                        tall(n, c0 + hd // 2 - 1, hT, hd % 2)
                    if hd == SBH - 3:
                        gla_keys(n0 + B_KD)
                    elif hd == SBH - 2:
                        gla_scores(n0 + B_GS)
                own_copies(n0 + B_KD, 2)
                gla_sums(n0 + B_KV, (n0 + B_GV, n0 + B_GV1))
                own_copies(v0, NBLK)
                stick_out(n0 + B_SO)

            def gate_input(n):
                w = claim_bank(pe, n)
                pe.wait_ge(consts_in, 16 * N_CONSTS)
                for k in range(KT):
                    last = nc.tensor.matmul(w[0:RANK, 0:T], w_rank[:, k, :], hT[:, k, :], start=(k == 0), stop=(k == KT - 1))
                last.then_inc(full[n % WB], 1)

            def gate_logits(n):
                w = claim_bank(pe, n)
                for j in range(2):
                    last = nc.tensor.matmul(w[:, j * T:(j + 1) * T], w_alpha[:, j * P:(j + 1) * P], alphaT[:, :],
                                            start=True, stop=True)
                last.then_inc(full[n % WB], 1)

            def gla_keys(n0):
                pe.wait_ge(gla_in, 1)
                for k in range(2):
                    w = claim_bank(pe, n0 + k)
                    pairs = [(c, j) for c in ((0, 1) if k == 0 else (2,)) for j in range(2)]
                    for at, (c, j) in enumerate(pairs):
                        last = transpose(w[:, at * P:(at + 1) * P], kdz[:, c, j, :])
                    last.then_inc(full[(n0 + k) % WB], 1)

            def gla_sums(n0, values):
                for c in range(3):
                    own_copies(values[c // 2], 1)
                    w = claim_bank(pe, n0 + c)
                    for j in range(2):
                        last = nc.tensor.matmul(w[:, j * T:(j + 1) * T], kd[:, c, j, :],
                                                v_g[:, c // 2, j * T:(j + 1) * T], start=True, stop=True)
                    last.then_inc(full[(n0 + c) % WB], 1)

            def gla_scores(n0):
                for b in range(NBLK):
                    w = claim_bank(pe, n0 + b)
                    for hd in range(GH):
                        last = nc.tensor.matmul(w[:, hd * P:(hd + 1) * P], kin[:, hd // 2, b * P:(b + 1) * P],
                                                qz[:, hd, b * P:(b + 1) * P], start=True, stop=True)
                    last.then_inc(full[(n0 + b) % WB], 1)

            def gla_out(n0):
                pe.wait_ge(gla_states, 3)
                pe.wait_ge(scores_masked, 2 * NBLK)
                for b in range(NBLK):
                    w = claim_bank(pe, n0 + b)
                    for hd in range(GH):
                        cols = slice(hd * GDV, (hd + 1) * GDV)
                        nc.tensor.matmul(w[:, cols], scT[:, b, hd, :], v_g[:, b, cols], start=True, stop=True)
                        for c in (2 * b, 2 * b + 1):
                            if c:
                                at = c % 2 * GC
                                last = nc.tensor.matmul(w[at:at + GC, cols], qz[:, hd, c * GC:(c + 1) * GC],
                                                        state[:, c - 1, hd // 2, :], start=False, stop=True,
                                                        skip_group_check=True)
                    last.then_inc(full[(n0 + b) % WB], 1)

            def stick_score(n, hd):
                w = claim_bank(pe, n)
                nc.tensor.matmul(w[:, 0:T], kz[:, hd, 0:P], qT[:, hd // 2, :], start=True, stop=True)
                nc.tensor.matmul(w[:, T:T + P], kz[:, hd, P:T], qT[:, hd // 2, P:T], start=True, stop=True)\
                    .then_inc(full[n % WB], 1)

            def stick_exponent(n, hd):
                w = claim_bank(pe, n)
                pe.wait_ge(log_ready, hd + 1)
                s = stick[:, 1, hd % 2, :]
                nc.tensor.matmul(w[:, 0:T], kz[:, hd, 0:P], qT[:, hd // 2, :], start=True, stop=False)
                nc.tensor.matmul(w[:, 0:T], suffix[:, 0, :], s[:, 0:T], start=False, stop=False)
                nc.tensor.matmul(w[:, P:T], suffix[:, 1, :], s[:, T:T + P], start=False, stop=True)
                nc.tensor.matmul(w[:, T:T + P], kz[:, hd, P:T], qT[:, hd // 2, P:T], start=True, stop=False)
                nc.tensor.matmul(w[:, T:T + P], suffix[:, 0, :], s[:, T:T + P], start=False, stop=True)\
                    .then_inc(full[n % WB], 1)

            def stick_out(n0):
                pe.wait_ge(prob_ready, SBH)
                for k in range(2):
                    n = n0 + k
                    w = claim_bank(pe, n)
                    for j in range(2):
                        for r in range(2):
                            hd = 4 * k + 2 * j + r
                            rows, cols = slice(64 * r, 64 * r + 64), slice(hd * SBD, (hd + 1) * SBD)
                            nc.tensor.matmul(w[rows, j * T:(j + 1) * T], v_sb[:, 0, cols], AT[:, hd, 0:T],
                                             start=True, stop=False)
                            last = nc.tensor.matmul(w[rows, j * T + P:(j + 1) * T], v_sb[:, 1, cols], AT[:, hd, T:T + P],
                                                    start=False, stop=True)
                    last.then_inc(full[n % WB], 1)

            pe.sem_inc(v_used, 2)
            pe.wait_ge(masks, IDENT_MASKS)
            for kind, args, at in walk():
                bank, chunk = at.bank, at.chunk
                if kind == "PROJQK":
                    for k in range(2):
                        wide(bank + 2 * k, await_chunk(pe, chunk + k), slice(0, T))
                elif kind == "PROJV":
                    for b in range(NBLK):
                        tall(bank + b, chunk, hT, b)
                elif kind == "MIX0":
                    mix0(bank, chunk, at.banks["PROJV",])
                elif kind == "GLAREAD":
                    gla_out(bank)
                elif kind == "GAINS":
                    pe.wait_ge(gain_rows_in, 32)
                    w = claim_bank(pe, bank)
                    nc.tensor.matmul(w[:, 0:N_GAINS], gain_rows[:, :], ident[0:N_GAINS, 0:N_GAINS], is_transpose=True,
                                     start=True, stop=True).then_inc(full[bank % WB], 1)
                elif kind == "STICK0":
                    own_copies(at.banks["PROJQK",], 4)
                    stick_score(bank, 0)
                elif kind == "GLAOUT":
                    b = args[0]
                    own_copies(at.banks["GLAREAD",] + b, 1)
                    fill_transposed(bank, og[:, b, :])
                elif kind == "OUT":
                    b, n, kh = args
                    if kh:
                        own_copies(at.banks["GLAOUT", b], 1)
                    else:
                        own_copies(at.banks["MIX0",] + B_SO, 2)
                    wt = await_chunk(pe, at.chunk - 2 + n)
                    for k in range(kh * KT // 2, (kh + 1) * KT // 2):
                        last = nc.tensor.matmul(acc[2 * b + n][:, :], mixT[:, k, b * P:(b + 1) * P], wt[:, k, :],
                                                start=(k == 0), stop=(k == KT - 1))
                    if kh:
                        last.then_inc(out_full, 1)
                elif kind == "SPATIAL":
                    pe.wait_ge(nat_masked, 1)
                    for k in range(2):
                        fill_transposed(bank + k, nat[:, 4 * k * P:4 * (k + 1) * P])
                elif kind == "TRANSPOSE":
                    for k, b in enumerate(args[0]):
                        make_hT(bank + 2 * k, b)
                elif kind == "QKEYS":
                    pe.wait_ge(nat_in, 16 * (at.nat + 1))
                    for k in range(4):
                        fill_transposed(bank + k, nat[:, 4 * k * NK:4 * (k + 1) * NK])
                elif kind == "HTAKE":
                    own_copies(bank, 2 * len(args[0]))
                elif kind == "QPROD":
                    if in_place_of_its_own(kind, args):
                        pe.wait_ge(first_chunk_in, 16)
                        wt = first_chunk
                    else:
                        wt = await_chunk(pe, chunk)
                    for k, b in enumerate(args[1]):
                        wide(bank + k, wt, slice(b * P, (b + 1) * P), range(2 * args[3][0], 2 * args[3][-1] + 2))
                elif kind == "QDOT":
                    layer, blocks, m, heads = args
                    own_copies(at.banks["QKEYS", layer], 4)
                    for k, b in enumerate(blocks):
                        q = at.banks["QPROD", *args] + k
                        own_copies(q, 1)
                        w = claim_bank(pe, bank + k)
                        for t in range(2 * len(heads)):
                            last = nc.tensor.matmul(w[:, t * P:(t + 1) * P], queries[:, q % 3, t * P:(t + 1) * P],
                                                    keysT[:, 4 * m + 2 * heads[0] + t, :], start=True, stop=True)
                        last.then_inc(full[(bank + k) % WB], 1)
                elif kind == "ACC":
                    layer, b = args
                    pe.wait_ge(x_ready, at.x_writes)
                    for n in range(2):
                        nc.tensor.matmul(acc[2 * b + n][:, :], ident[:, :], x[:, b, n * CH:(n + 1) * CH],
                                         start=True, stop=True)
                elif kind == "GATHER":
                    layer, b, i0, i1 = args
                    t0 = gather_turn(layer, b)
                    with pe.Fori(i0, i1) as i:
                        for k in range(STEPS):
                            g = k // HALF
                            if k % HALF == 0:
                                pe.wait_ge(diag_ready, 2 * (t0 + i) + g + 1)
                            pe.wait_ge(v_in[k], 16 * (t0 + i + 1))
                            for n in range(2):
                                last = nc.tensor.matmul(acc[2 * b + n][:, :], diag[:, k, :],
                                                        ring[:, STEPS + k, n * CH:(n + 1) * CH],
                                                        start=False, stop=True, skip_group_check=True)
                            if k % HALF == HALF - 1:
                                last.then_inc(v_used, 1)
                elif kind == "ZPROJ":
                    tall(bank, chunk, hT, args[0])
                elif kind == "MIXG":
                    b, k = args
                    own_copies(at.banks["SPATIAL",], 2)
                    pe.wait_ge(v_ready, b + 1)
                    w = claim_bank(pe, bank)
                    for g in (2 * k, 2 * k + 1):
                        last = nc.tensor.matmul(w[:, g % 2 * SGC:(g % 2 + 1) * SGC], spatialT[:, g, :],
                                                z[:, SGW + g * SGC:SGW + (g + 1) * SGC], start=True, stop=True)
                    last.then_inc(full[bank % WB], 1)
                elif kind == "MIXT":
                    b, k = args
                    own_copies(at.banks["MIXG", b, k], 1)
                    fill_transposed(bank, z[:, k * CH:(k + 1) * CH])
                elif kind == "MIXO":
                    b, n = args
                    w = claim_bank(pe, bank)
                    for kh in range(2):
                        for k in (2 * kh, 2 * kh + 1):
                            own_copies(at.banks["MIXT", b, k], 1)
                        wt = await_chunk(pe, chunk + kh)
                        for k in range(KT):
                            last = nc.tensor.matmul(w[:, :], mixT1[:, kh * KT + k, :], wt[:, k, :],
                                                    start=(kh + k == 0), stop=(kh == 1 and k == KT - 1))
                        last.then_inc(full[bank % WB] if kh else half_used, 1)


_INS = ["x", "norm_mix", "norm_ffn", "ab_w_in", "ab_w_alpha2", "ab_b_alpha2", "ab_gla_norm", "ab_w_out",
        "c_w_in", "c_v_norm", "c_w_spatial", "c_b_spatial", "c_w_out", "peer_w_q", "peer_subkeys",
        "peer_u", "peer_v", "final_norm"]


def kernel(**inputs):
    import numpy as _np
    import concourse.bacc as _bacc
    from concourse import mybir as _mybir
    from concourse.bass_utils import run_bass_kernel_spmd as _run

    nc = _bacc.Bacc("TRN2", target_bir_lowering=False, num_devices=1)
    arrays, args = {}, []
    for name in _INS:
        a = _np.ascontiguousarray(inputs[name])
        arrays[f"in_{name}"] = a
        args.append(nc.dram_tensor(f"in_{name}", a.shape, _mybir.dt.from_np(a.dtype), kind="ExternalInput").ap())
    out = nc.dram_tensor("out", (1, T, D), _mybir.dt.float32, kind="ExternalOutput").ap()
    trunk(nc, *args, out)
    r = _run(nc, [arrays], core_ids=[0])
    return r.results[0]["out"]
```
